# Optimizing a Trainium2 kernel written in Bass

```python
import jax, jax.numpy as jnp
from jax import lax
import numpy as np

D_MODEL = 1024
BATCH = 1
SEQ = 512
DEPTH = 2

GRID_W = 64
CTX_LEN = 256
EPS = 1e-6

N_Q_HEADS = 8
N_KV_HEADS = 2
HEAD_DIM = 64
ATTN_WIDTH = N_Q_HEADS * HEAD_DIM
KV_WIDTH = N_KV_HEADS * HEAD_DIM
QKV_WIDTH = ATTN_WIDTH + 2 * KV_WIDTH
Q_BLOCK = 128
ROPE_THETA = 10000.0

CHUNK = 128
GMLP_GROUPS = 4
GMLP_WIDTH = D_MODEL // 4

CONV_WIDTH = D_MODEL // 4
CONV_K = 31

MIX_WIDTH = ATTN_WIDTH + GMLP_WIDTH + CONV_WIDTH
IN_WIDTH = QKV_WIDTH + 2 * GMLP_WIDTH + 2 * CONV_WIDTH

PEER_HEADS = 8
N_KEYS = 128
N_EXPERTS = N_KEYS * N_KEYS
PEER_TOPK = 16
PEER_QDIM = 256
PEER_TOKEN_BLOCK = 128

ALPHA = (2 * DEPTH) ** 0.25
BETA = (8 * DEPTH) ** -0.25

kernel_name = "hybrid_parallel_heads_peer_dit_block"

def layer_norm(x, g=None, b=None):
    xf = x.astype(jnp.float32)
    mu = jnp.mean(xf, -1, keepdims=True)
    var = jnp.mean(jnp.square(xf - mu), -1, keepdims=True)
    y = (xf - mu) * lax.rsqrt(var + EPS)
    if g is not None:
        y = y * g + b
    return y.astype(x.dtype)

def rms_norm(x, g):
    xf = x.astype(jnp.float32)
    y = xf * lax.rsqrt(jnp.mean(jnp.square(xf), -1, keepdims=True) + EPS) * g
    return y.astype(x.dtype)

def rope_1d(x, pos):
    half = x.shape[-1] // 2
    freqs = ROPE_THETA ** (-jnp.arange(half, dtype=jnp.float32) / half)
    ang = pos.astype(jnp.float32)[:, None] * freqs
    cos = jnp.cos(ang)[None, :, None, :]
    sin = jnp.sin(ang)[None, :, None, :]
    x1 = x[..., :half].astype(jnp.float32)
    x2 = x[..., half:].astype(jnp.float32)
    return jnp.concatenate([x1 * cos - x2 * sin, x1 * sin + x2 * cos], -1).astype(x.dtype)

def axial_rope(x, rows, cols):
    h = x.shape[-1] // 2
    return jnp.concatenate([rope_1d(x[..., :h], rows), rope_1d(x[..., h:], cols)], -1)

def modulation(cond, w_mod, b_mod):
    m = jax.nn.silu(cond) @ w_mod + b_mod
    return jnp.split(m, 6, axis=-1)

def modulate(x, shift, scale):
    return layer_norm(x) * (1.0 + scale) + shift

def attn_queries(p, q_g, rows=None, cols=None):
    B, L, _ = p.shape
    q = rms_norm(p[..., :ATTN_WIDTH].reshape(B, L, N_Q_HEADS, HEAD_DIM), q_g)
    return q if rows is None else axial_rope(q, rows, cols)

def attn_keys_values(p, k_g, rows=None, cols=None):
    B, L, _ = p.shape
    k = rms_norm(p[..., ATTN_WIDTH:ATTN_WIDTH + KV_WIDTH].reshape(B, L, N_KV_HEADS, HEAD_DIM), k_g)
    v = p[..., ATTN_WIDTH + KV_WIDTH:QKV_WIDTH].reshape(B, L, N_KV_HEADS, HEAD_DIM)
    if rows is not None:
        k = axial_rope(k, rows, cols)
    return k, v

def gqa_attend(q, k, v):
    B, Lq = q.shape[:2]
    qg = q.reshape(B, Lq, N_KV_HEADS, N_Q_HEADS // N_KV_HEADS, HEAD_DIM)
    s = jnp.einsum('bqgrd,bkgd->bgrqk', qg, k, preferred_element_type=jnp.float32) * (HEAD_DIM ** -0.5)
    pr = jax.nn.softmax(s, axis=-1).astype(v.dtype)
    o = jnp.einsum('bgrqk,bkgd->bqgrd', pr, v)
    return o.reshape(B, Lq, ATTN_WIDTH)

def blocked_attention(q, k, v):
    B, L = q.shape[:2]
    nb = L // Q_BLOCK
    qb = jnp.moveaxis(q.reshape(B, nb, Q_BLOCK, N_Q_HEADS, HEAD_DIM), 1, 0)
    ob = lax.map(lambda qi: gqa_attend(qi, k, v), qb)
    return jnp.moveaxis(ob, 0, 1).reshape(B, L, ATTN_WIDTH)

def chunk_gmlp(z, ln_g, ln_b, w_s, b_s):
    B, L, _ = z.shape
    z = jax.nn.gelu(z)
    u, v = jnp.split(z, 2, axis=-1)
    v = layer_norm(v, ln_g, ln_b)
    v = v.reshape(B, L // CHUNK, CHUNK, GMLP_GROUPS, GMLP_WIDTH // GMLP_GROUPS)
    s = jnp.einsum('gpq,bnqgc->bnpgc', w_s, v) + b_s.T[None, None, :, :, None]
    return u * s.reshape(B, L, GMLP_WIDTH)

def conformer_conv(z, w_dw, b_dw, ln_g, ln_b, w_pw, b_pw):
    a, g = jnp.split(z, 2, axis=-1)
    y = a * jax.nn.sigmoid(g)
    y = lax.conv_general_dilated(
        y, w_dw[:, None, :], window_strides=(1,),
        padding=[(CONV_K // 2, CONV_K // 2)],
        dimension_numbers=('NWC', 'WIO', 'NWC'),
        feature_group_count=CONV_WIDTH) + b_dw
    y = jax.nn.silu(layer_norm(y, ln_g, ln_b))
    return y @ w_pw + b_pw

def token_mixers(p, attn_o, gmlp_ln_g, gmlp_ln_b, gmlp_w_s, gmlp_b_s,
                 conv_w_dw, conv_b_dw, conv_ln_g, conv_ln_b, conv_w_pw, conv_b_pw, w_out):
    zg = p[..., QKV_WIDTH:QKV_WIDTH + 2 * GMLP_WIDTH]
    zc = p[..., QKV_WIDTH + 2 * GMLP_WIDTH:]
    y_g = chunk_gmlp(zg, gmlp_ln_g, gmlp_ln_b, gmlp_w_s, gmlp_b_s)
    y_c = conformer_conv(zc, conv_w_dw, conv_b_dw, conv_ln_g, conv_ln_b, conv_w_pw, conv_b_pw)
    return jnp.concatenate([attn_o, y_g, y_c], axis=-1) @ w_out

def peer_ffn(h, w_q, sub_keys, u_tab, v_tab):
    B, L, D = h.shape
    hb = h.reshape(-1, PEER_TOKEN_BLOCK, D)

    def block(xb):
        T = xb.shape[0]
        q = (xb @ w_q).reshape(T, PEER_HEADS, 2, PEER_QDIM // 2)
        s = jnp.einsum('thpd,hpkd->thpk', q, sub_keys, preferred_element_type=jnp.float32)
        s_top, i_top = lax.top_k(s, PEER_TOPK)
        cand = s_top[:, :, 0, :, None] + s_top[:, :, 1, None, :]
        cand_idx = i_top[:, :, 0, :, None] * N_KEYS + i_top[:, :, 1, None, :]
        best, pos = lax.top_k(cand.reshape(T, PEER_HEADS, PEER_TOPK * PEER_TOPK), PEER_TOPK)
        experts = jnp.take_along_axis(cand_idx.reshape(T, PEER_HEADS, -1), pos, axis=-1)
        gate = jax.nn.softmax(best, axis=-1)
        act = jax.nn.gelu(jnp.einsum('thkd,td->thk', u_tab[experts], xb,
                                     preferred_element_type=jnp.float32))
        w = (gate * act).astype(xb.dtype)
        return jnp.einsum('thk,thkd->td', w, v_tab[experts])

    return lax.map(block, hb).reshape(B, L, D)

def setup_inputs(seed: int = 0) -> dict:
    key = jax.random.key(seed)
    ks = jax.random.split(key, 28)
    D = D_MODEL

    def nrm(i, shape, s):
        return jax.random.normal(ks[i], shape, jnp.float32) * s

    def gain(i, shape):
        return 1.0 + nrm(i, shape, 0.01)

    return {
        "x": nrm(0, (BATCH, SEQ, D), 1.0),
        "c": nrm(1, (BATCH, D), 1.0),
        "ctx": nrm(2, (BATCH, CTX_LEN, D), 1.0),
        "c_ctx": nrm(3, (D,), 1.0),
        "w_mod": nrm(4, (DEPTH, D, 6 * D), 0.5 * D ** -0.5),
        "b_mod": nrm(5, (DEPTH, 6 * D), 0.01),
        "w_in": nrm(6, (DEPTH, D, IN_WIDTH), D ** -0.5),
        "q_norm_g": gain(7, (DEPTH, HEAD_DIM)),
        "k_norm_g": gain(8, (DEPTH, HEAD_DIM)),
        "gmlp_ln_g": gain(9, (DEPTH, GMLP_WIDTH)),
        "gmlp_ln_b": nrm(10, (DEPTH, GMLP_WIDTH), 0.01),
        "gmlp_w_s": nrm(11, (DEPTH, GMLP_GROUPS, CHUNK, CHUNK), CHUNK ** -0.5),
        "gmlp_b_s": gain(12, (DEPTH, GMLP_GROUPS, CHUNK)),
        "conv_w_dw": nrm(13, (DEPTH, CONV_K, CONV_WIDTH), CONV_K ** -0.5),
        "conv_b_dw": nrm(14, (DEPTH, CONV_WIDTH), 0.01),
        "conv_ln_g": gain(15, (DEPTH, CONV_WIDTH)),
        "conv_ln_b": nrm(16, (DEPTH, CONV_WIDTH), 0.01),
        "conv_w_pw": nrm(17, (DEPTH, CONV_WIDTH, CONV_WIDTH), CONV_WIDTH ** -0.5),
        "conv_b_pw": nrm(18, (DEPTH, CONV_WIDTH), 0.01),
        "w_out": nrm(19, (DEPTH, MIX_WIDTH, D), BETA * MIX_WIDTH ** -0.5),
        "ln1_g": gain(20, (DEPTH, D)),
        "ln1_b": nrm(21, (DEPTH, D), 0.01),
        "ln2_g": gain(22, (DEPTH, D)),
        "ln2_b": nrm(23, (DEPTH, D), 0.01),
        "peer_w_q": nrm(24, (DEPTH, D, PEER_HEADS * PEER_QDIM), D ** -0.5),
        "peer_sub_keys": nrm(25, (DEPTH, PEER_HEADS, 2, N_KEYS, PEER_QDIM // 2), (PEER_QDIM // 2) ** -0.5),
        "peer_u": nrm(26, (DEPTH, N_EXPERTS, D), D ** -0.5),
        "peer_v": nrm(27, (DEPTH, N_EXPERTS, D), BETA),
    }

def reference(x, c, ctx, c_ctx, w_mod, b_mod, w_in, q_norm_g, k_norm_g,
              gmlp_ln_g, gmlp_ln_b, gmlp_w_s, gmlp_b_s,
              conv_w_dw, conv_b_dw, conv_ln_g, conv_ln_b, conv_w_pw, conv_b_pw,
              w_out, ln1_g, ln1_b, ln2_g, ln2_b,
              peer_w_q, peer_sub_keys, peer_u, peer_v):
    B, L, _ = x.shape
    rows = L // GRID_W
    row_ids = jnp.repeat(jnp.arange(rows, dtype=jnp.int32), GRID_W)
    col_ids = jnp.arange(rows * GRID_W, dtype=jnp.int32) % GRID_W

    x_lat, x_ctx = x, ctx
    for l in range(DEPTH):
        last = l == DEPTH - 1
        sh1, sc1, g1, sh2, sc2, g2 = modulation(c[:, None, :], w_mod[l], b_mod[l])
        csh1, csc1, cg1, csh2, csc2, cg2 = modulation(c_ctx, w_mod[l], b_mod[l])
        mix_params = (gmlp_ln_g[l], gmlp_ln_b[l], gmlp_w_s[l], gmlp_b_s[l],
                      conv_w_dw[l], conv_b_dw[l], conv_ln_g[l], conv_ln_b[l],
                      conv_w_pw[l], conv_b_pw[l], w_out[l])

        p_lat = modulate(x_lat, sh1, sc1) @ w_in[l]
        p_ctx = modulate(x_ctx, csh1, csc1) @ w_in[l]
        k_c, v_c = attn_keys_values(p_ctx, k_norm_g[l])
        k_l, v_l = attn_keys_values(p_lat, k_norm_g[l], row_ids, col_ids)
        q_l = attn_queries(p_lat, q_norm_g[l], row_ids, col_ids)
        k_all = jnp.concatenate([k_c, k_l], axis=1)
        v_all = jnp.concatenate([v_c, v_l], axis=1)
        o_lat = blocked_attention(q_l, k_all, v_all)
        y_lat = token_mixers(p_lat, o_lat, *mix_params)
        x_lat_new = layer_norm(ALPHA * x_lat + g1 * y_lat, ln1_g[l], ln1_b[l])

        f_lat = peer_ffn(modulate(x_lat_new, sh2, sc2), peer_w_q[l], peer_sub_keys[l], peer_u[l], peer_v[l])
        x_lat_new = layer_norm(ALPHA * x_lat_new + g2 * f_lat, ln2_g[l], ln2_b[l])

        if not last:
            q_c = attn_queries(p_ctx, q_norm_g[l])
            o_ctx = gqa_attend(q_c, k_c, v_c)
            y_ctx = token_mixers(p_ctx, o_ctx, *mix_params)
            x_ctx = layer_norm(ALPHA * x_ctx + cg1 * y_ctx, ln1_g[l], ln1_b[l])
            f_ctx = peer_ffn(modulate(x_ctx, csh2, csc2), peer_w_q[l], peer_sub_keys[l], peer_u[l], peer_v[l])
            x_ctx = layer_norm(ALPHA * x_ctx + cg2 * f_ctx, ln2_g[l], ln2_b[l])
        x_lat = x_lat_new
    return x_lat


_drawn_inputs = setup_inputs


def setup_inputs(seed=0):
    import zlib

    import numpy as np

    out = dict(_drawn_inputs(seed))
    spreads = {}
    factors = {'ctx': 27.198,
     'c_ctx': 11.928,
     'b_mod': 4.869,
     'q_norm_g': 200.0,
     'k_norm_g': 200.0,
     'gmlp_ln_g': 200.0,
     'gmlp_ln_b': 200.0,
     'gmlp_b_s': 200.0,
     'conv_b_dw': 8.0,
     'conv_ln_g': 200.0,
     'conv_ln_b': 200.0,
     'conv_b_pw': 200.0,
     'ln1_g': 48.551,
     'ln1_b': 48.973,
     'ln2_g': 52.858,
     'ln2_b': 55.133,
     'peer_w_q': 8.0,
     'peer_sub_keys': 8.0,
     'peer_u': 8.0,
     'peer_v': 8.0}
    for name, (base, spread) in spreads.items():
        noise = np.random.default_rng([zlib.crc32(name.encode()), seed]).standard_normal(out[name].shape)
        drawn = base * np.exp(spread * noise) if base else spread * noise
        out[name] = __import__('jax').numpy.asarray(drawn.astype(out[name].dtype))
    for name, factor in factors.items():
        out[name] = (out[name] * factor).astype(out[name].dtype)
    return out
```

```python
from contextlib import ExitStack

import concourse.bass as bass
from concourse import mybir

ALU = mybir.AluOpType
ACT = mybir.ActivationFunctionType
AX_X = mybir.AxisListType.X
F32 = mybir.dt.float32
U32 = mybir.dt.uint32

P = 128
D = 1024
KD = D // P
DEPTH = 2
LAT, CTXL = 512, 256
NLAT, NCTX = LAT // P, CTXL // P
NB = NLAT + NCTX
TOK = LAT + CTXL
EPS = 1e-6
HD = 64
NQ, NKV = 8, 2
REP = NQ // NKV
AW, KW = NQ * HD, NKV * HD
QKV = AW + 2 * KW
GW = D // 4
CW = D // 4
GROUPS = 4
GC = GW // GROUPS
TAPS = 31
PAD = TAPS // 2
IN_W = QKV + 2 * GW + 2 * CW
U_AT, V_AT = QKV, QKV + GW
A_AT, G_AT = QKV + 2 * GW, QKV + 2 * GW + CW
PH = 8
NK = 128
TOPK = 16
NEXP = NK * NK
SLOTS = PH * TOPK
ALPHA = float((2 * DEPTH) ** 0.25)
SCALE = float(HD ** -0.5)
LOWEST = -3.0e38
MODC = 6 * D // 512
INC, INW = 4, IN_W // 4
OUTC = D // 512
QC = 2 * PH * P // 512
WCHUNKS = MODC + INC + OUTC + QC
UR = 8
BLOCKS = [NB, NLAT]
PEER = [(0, NB), (1, NLAT)]


class Chain:

    def __init__(self, eng, sem, base=0):
        self.eng, self.sem, self.base, self.n, self.counts = eng, sem, base, 0, {}

    def __call__(self, ins):
        ins.then_inc(self.sem, 1)
        self.n += 1
        self.eng.wait_ge(self.sem, self.base + self.n)

    def sig(self, ins, sem):
        ins.then_inc(sem, 1)
        self.counts[sem.name] = self.counts.get(sem.name, 0) + 1
        self.eng.wait_ge(sem, self.counts[sem.name])


PER_BLOCK = {"g_idx": PH, "g_ud": SLOTS, "g_gel": PH, "g_w": PH, "g_dg": SLOTS, "g_vd": SLOTS, "g_y": 2, "g_best": PH,
             "g_h": 1, "lo_sig": 1, "lo_gelu": 1, "lo_glu": 1, "lo_gt": 1, "lo_cin": 1, "lo_vn": 1, "lo_gm": 1, "lo_yg": 1, "lo_ygt": 1,
             "lo_yge": 1, "lo_ct": 1, "lo_cy": 1, "lo_cn": 1, "lo_silu": 1, "lo_st": 1, "lo_se": 1, "ph_h": 1, "ph_tr": 1, "ph_hev": 2,
             "ou_mm": OUTC, "ou_ev": OUTC, "q_tk": 2 * PH}


def top_steps(block0):
    if block0:
        return {1: [(0, 2), (0, 3)], 2: [(0, 4), (0, 5)], 3: [(0, 6), (0, 7)], 4: [(1, 0), (1, 1)], 5: [(1, 2), (1, 3)],
                6: [(1, 4)], 7: [(1, 5)], 8: [(1, 6)]}
    return {h: [(0, PH - 1)] if h == 1 else [(1, h - 2)] for h in range(1, PH + 1)}


PER_LAYER = {"bmod": 16, "mod_mm": MODC, "mod_ev": MODC, "mod_st": 16, "mbc_in": 64, "gqk": 32, "row_ld": 64, "lo_ld": 96, "mbc_out": 32,
             "mbc_sc2": 32, "mbc_sh2": 32, "mbc_g2": 32, "lnbc": 32, "lnbc2": 32, "sk_ld": 16, "in_h": NB, "in_tr": NB, "in_hev": 2 * NB,
             "at_q": NB, "at_tr": NB, "at_qev": NB, "q_mm": 2 * PH, "q_ev": 2 * PH, "q_s": 2 * PH, "sk_tr": 4, "sk_ev": 4}


class Signals:

    def __init__(self, layer, sems):
        self.layer, self.sems = layer, sems

    def __getitem__(self, name):
        return self.sems[name]

    def at(self, name, count):
        before = PER_BLOCK.get(name, 0) * sum(BLOCKS[:self.layer]) + PER_LAYER.get(name, 0) * self.layer
        return self.sems[name], before + count


def chunk_number(layer, kind, i):
    first = {"mod": 0, "in": MODC, "out": MODC + INC, "q": MODC + INC + OUTC}[kind]
    return layer * WCHUNKS + first + i


def in_tiles(layer):
    return [(c, t) for c in range(INC) for t in range(NB) if t < BLOCKS[layer] or (c * INW < AW + 2 * KW and (c + 1) * INW > AW)]


def in_owner(tile):
    c, t = tile
    return "dve" if c == 1 and t % 2 else "act"


def att_units(layer):
    units = [(0, NLAT, h, t) for h in range(NQ) for t in range(NLAT)]
    if BLOCKS[layer] == NB:
        units += [(NLAT, NCTX, h, t) for h in range(NQ) for t in range(NLAT, NB)]
    return units


def build(nc, a, rope_cos, rope_sin, out, debug=None):
    with ExitStack() as ctx:
        def sb(name, shape, dt=F32):
            return ctx.enter_context(nc.sbuf_tensor(name, shape, dt))

        def sem(name):
            return ctx.enter_context(nc.semaphore(name))

        X = sb("X", [P, NB, D])
        hT = sb("hT", [P, KD, TOK])
        W = sb("W", [P, 2, KD * 512])
        modbc = sb("modbc", [P, 2, 2, D])
        lnbc = sb("lnbc", [P, 2, D])
        ident = sb("ident", [P, P])
        iota16 = sb("iota16", [P, TOPK])
        cosT = sb("cosT", [P, NLAT, 2, 16])
        sinT = sb("sinT", [P, NLAT, 2, 16])
        cond = sb("cond", [P, 2, KD])
        eps = sb("eps", [P, 1])
        st = sb("st", [P, NB, 2, 6])
        mv = sb("mv", [P, NB, 2])
        sd = sb("sd", [P, NB * 10])
        rstd = sb("rstd", [P, NB * 10])
        tiny = sb("tiny", [P, 16])
        gsum = sb("gsum", [P, PH])
        cols = sb("cols", [P, GROUPS + 2 * (TAPS + 2)])
        ARENA = 25472
        arena = sb("arena", [P, ARENA])
        PS = ctx.enter_context(nc.psum_tensor("PS", [P, 8, 512], F32))
        PSf = PS[:, :, :].rearrange("p b n -> p (b n)")
        modd = nc.dram_tensor("modd", (DEPTH, 2, 6 * D), F32).ap()

        def carve(*spec):
            at, views = 0, []
            for dims in spec:
                n = 1
                for x in dims:
                    n *= x
                v = arena[:, at:at + n]
                at += n
                if len(dims) == 2:
                    v = v.rearrange("p (a b) -> p a b", a=dims[0])
                if len(dims) == 3:
                    v = v.rearrange("p (a b c) -> p a b c", a=dims[0], b=dims[1])
                views.append(v)
            assert at <= ARENA, at
            return views

        wv = [W[:, s, :].rearrange("p (k n) -> p k n", k=KD) for s in range(2)]
        modrow, bmod = carve([6 * D], [6 * D])
        MIX = [NB, IN_W], [REP, TOK], [TOK]
        proj, hb = carve([NB, IN_W], [2, D])
        _, qT, kT, probs, probsT, cin, cacc = carve(*MIX, [2, TOK], [2, NB * LAT], [2, TOK + 4 * PAD], [2, TOK])
        _, _, _, qn, tA, tB, qr, gqk, rows, bsr = carve(*MIX, [10, HD], [320], [320], [NB, 10 * HD], [10, HD], [CW], [P])
        _, cy, sT, ws, wsT, wpw, gln, cln = carve([NB, IN_W], [NB, CW], [2, TOK], [GROUPS, P], [GROUPS, P], [2, CW], [2, GW], [2, CW])
        H2, V16, I16f, sk, skT, qs, scr, shift2, spare = carve([NB, D], [NB, 2 * PH * TOPK], [NB, 2 * PH * TOPK], [2 * PH, P], [2 * PH, P],
                                                               [2, TOK], [P], [2, D], [2, 512])
        _, _, _, vring, hcur, cand, eq, dg, best, gate, actv, gel, wgt, idxf, pos, hilo, e12 = carve(
            [NB, D], [NB, 2 * PH * TOPK], [NB, 2 * PH * TOPK], [UR, D], [D], [TOPK * TOPK], [TOPK * TOPK], [4, P],
            [SLOTS], [SLOTS], [SLOTS], [SLOTS], [SLOTS], [SLOTS], [TOPK], [2 * TOPK], [2 * TOPK])
        I16 = I16f.bitcast(U32)
        idx = idxf.bitcast(U32)
        pos = pos.bitcast(U32)
        hilo = hilo.bitcast(U32)
        uring = W[:, :, :].rearrange("p s (r d) -> p (s r) d", d=D)
        H2f = H2.rearrange("p b d -> p (b d)")
        V16f = V16.rearrange("p b n -> p (b n)")
        I16f = I16.rearrange("p b n -> p (b n)")

        s_phase = sem("s_phase")
        s_const = sem("s_const")
        s_eps = sem("s_eps")
        s_load0 = sem("s_load0")
        s_cond = sem("s_cond")
        s_wfull = [sem(f"s_wfull{i}") for i in range(2)]
        c_dve = sem("c_dve")
        c_pool = sem("c_pool")
        c_act = sem("c_act")
        s_out = sem("s_out")
        names = ["bmod", "mod_mm", "mod_ev", "mod_st", "mbc_in", "stat", "root", "in_h", "in_tr", "in_hev", "in_mm", "in_eva", "in_evd",
                 "gqk", "row_ld", "mbc_out", "mbc_sc2", "lnbc", "at_q", "at_tr", "at_qev", "at_s", "at_max", "at_exp", "at_rcp", "at_nrm", "at_t", "at_tev",
                 "at_pv", "at_oev", "lo_ld", "lo_rt", "lo_rev", "lo_wt", "lo_wev", "lo_sig", "lo_gelu", "lo_glu", "lo_gt", "lo_cin", "lo_vn", "lo_gm",
                 "lo_yg", "lo_ygt", "lo_yge", "lo_tap", "lo_ct", "lo_cy", "lo_cn", "lo_silu", "lo_st", "lo_se", "lo_pw", "lo_pwe",
                 "ou_mm", "ou_ev", "mbc_sh2", "ph_h", "ph_tr", "ph_hev", "sk_ld", "sk_tr", "sk_ev", "q_mm", "q_ev", "q_s", "q_tk",
                 "g_idx", "g_ud", "g_gel", "g_w", "g_dg", "g_vd", "g_y", "g_best", "mbc_g2", "lnbc2", "ep", "g_h"]
        shared = {n: sem(n) for n in (*PER_BLOCK, *PER_LAYER)}
        S = [Signals(layer, {n: shared[n] if n in shared else sem(f"{n}_{layer}") for n in names}) for layer in range(DEPTH)]
        s_u = [sem(f"s_u{r}") for r in range(UR)]
        s_v = [sem(f"s_v{r}") for r in range(UR)]
        c_tk = sem("c_tk")
        s_hold = sem("s_hold")
        c_up = sem("c_up")
        passed = [sem(f"passed{i}") for i in range(2)]

        ENGINES = 4
        phases = [0]

        def phase_end(eng, n):
            eng.drain().then_inc(s_phase, 1)
            eng.wait_ge(s_phase, ENGINES * n)

        block = ctx.enter_context(nc.Block())

        @block.sync
        def _(sp):
            dma_count = [0, 0]

            def load(n, kind, src, width, free):
                slot = n % 2
                rows = src.rearrange("(p k) n -> p k n" if kind == "mod" else "(k p) n -> p k n", p=P)
                if free is not None:
                    sp.wait_ge(*free)
                sp.dma_start(wv[slot][:, :, 0:width], rows).then_inc(s_wfull[slot], 16)

            def done(layer, kind, i):
                q = S[layer]
                if kind == "mod":
                    return q.at("mod_mm", i + 1)
                if kind == "in":
                    return q.at("in_mm", max(n for n, (c, t) in enumerate(in_tiles(layer)) if c == i) + 1)
                if kind == "out":
                    return q.at("ou_mm", OUTC * (BLOCKS[layer] - 1) + i + 1)
                return q.at("q_mm", 4 * (i + 1))

            order = []
            for layer in range(DEPTH):
                order += [(layer, "mod", i, a["w_mod"][layer][:, i * 512:(i + 1) * 512], 512) for i in range(MODC)]
                order += [(layer, "in", i, a["w_in"][layer][:, i * INW:(i + 1) * INW], INW) for i in range(INC)]
                order += [(layer, "out", i, a["w_out"][layer][:, i * 512:(i + 1) * 512], 512) for i in range(OUTC)]
                order += [(layer, "q", i, a["peer_w_q"][layer][:, i * 512:(i + 1) * 512], 512) for i in range(QC)]
            for n, (layer, kind, i, src, width) in enumerate(order):
                assert n == chunk_number(layer, kind, i)
                if layer > 0 and kind == "mod" and i < 2:
                    free = S[layer - 1].at("g_ud", SLOTS * BLOCKS[layer - 1])
                else:
                    free = done(*order[n - 2][:3]) if n >= 2 else None
                load(n, kind, src, width, free)
            last = S[DEPTH - 1]
            sp.wait_ge(last["ep"], 1)
            sp.dma_start(out[0].rearrange("(b p) d -> p b d", p=P), X[:, 0:NLAT, :]).then_inc(s_out, 16)
            sp.wait_ge(s_out, 16)

        @block.gpsimd
        def _(pool):
            ch = Chain(pool, c_pool)
            ch(pool.iota(ident[:, :], [[1, P]], base=0, channel_multiplier=-1, allow_small_or_imprecise_dtypes=True))
            pool.iota(iota16[:, :], [[1, TOPK]], base=0, channel_multiplier=0, allow_small_or_imprecise_dtypes=True).then_inc(s_const, 1)
            pool.tensor_scalar(ident[:, :], ident[:, :], 0.0, None, ALU.is_equal).then_inc(s_const, 1)
            pool.dma_start(cond[:, 0, :], a["c"][0].rearrange("(p k) -> p k", p=P)).then_inc(s_load0, 16)
            pool.dma_start(cond[:, 1, :], a["c_ctx"].rearrange("(p k) -> p k", p=P)).then_inc(s_load0, 16)
            pool.dma_start(X[:, 0:NLAT, :], a["x"][0].rearrange("(b p) d -> p b d", p=P)).then_inc(s_load0, 16)
            pool.dma_start(X[:, NLAT:NB, :], a["ctx"][0].rearrange("(b p) d -> p b d", p=P)).then_inc(s_load0, 16)
            pool.dma_start(cosT[:, :, :, :].rearrange("p b a f -> p b (a f)"), rope_cos.rearrange("(b p) f -> p b f", p=P)).then_inc(s_load0, 16)
            pool.dma_start(sinT[:, :, :, :].rearrange("p b a f -> p b (a f)"), rope_sin.rearrange("(b p) f -> p b f", p=P)).then_inc(s_load0, 16)
            pool.wait_ge(s_load0, 96)

            def rows_to(dst, src, done):
                pool.dma_start(dst, src.partition_broadcast(P)).then_inc(done, 16)

            def modulation_row(layer, stream, part, slot, done):
                rows_to(modbc[:, stream, slot, :], modd[layer, stream, part * D:(part + 1) * D], done)

            n = 0
            for layer in range(DEPTH):
                q = S[layer]
                pool.dma_start(bmod[0:2, :], a["b_mod"][layer].partition_broadcast(2)).then_inc(q["bmod"], 16)
                pool.wait_ge(*q.at("mod_ev", MODC))
                pool.dma_start(modd[layer], modrow[0:2, :]).then_inc(q["mod_st"], 16)
                pool.wait_ge(*q.at("mod_st", 16))
                for stream in range(2):
                    for part in range(2):
                        modulation_row(layer, stream, part, part, q["mbc_in"])
                n += 1
                phase_end(pool, n)
                for dst, src in ((rows[0:TAPS, :], a["conv_w_dw"][layer]),
                                 (rows[TAPS:TAPS + 1, :], a["conv_b_dw"][layer:layer + 1, :]),
                                 (rows[TAPS + 1:TAPS + 2, :], a["conv_b_pw"][layer:layer + 1, :]),
                                 (bsr[0:GROUPS, :], a["gmlp_b_s"][layer])):
                    pool.dma_start(dst, src).then_inc(q["row_ld"], 16)
                pool.dma_start(gqk[:, 0:NQ, :], a["q_norm_g"][layer].partition_broadcast(P).unsqueeze(1).to_broadcast([P, NQ, HD])).then_inc(q["gqk"], 16)
                pool.dma_start(gqk[:, NQ:NQ + NKV, :], a["k_norm_g"][layer].partition_broadcast(P).unsqueeze(1).to_broadcast([P, NKV, HD])).then_inc(q["gqk"], 16)
                n += 1
                phase_end(pool, n)
                for stream in range(2):
                    modulation_row(layer, stream, 2, 0, q["mbc_out"])
                    modulation_row(layer, stream, 4, 1, q["mbc_sc2"])
                rows_to(lnbc[:, 0, :], a["ln1_g"][layer], q["lnbc"])
                rows_to(lnbc[:, 1, :], a["ln1_b"][layer], q["lnbc"])
                n += 1
                phase_end(pool, n)
                for dst, src in ((ws, a["gmlp_w_s"][layer].rearrange("g p q -> p g q")),
                                 (wpw, a["conv_w_pw"][layer].rearrange("(k p) n -> p k n", p=P))):
                    pool.dma_start(dst, src).then_inc(q["lo_ld"], 16)
                for dst, src in ((gln[:, 0, :], a["gmlp_ln_g"][layer]), (gln[:, 1, :], a["gmlp_ln_b"][layer]),
                                 (cln[:, 0, :], a["conv_ln_g"][layer]), (cln[:, 1, :], a["conv_ln_b"][layer])):
                    rows_to(dst, src, q["lo_ld"])
                n += 1
                phase_end(pool, n)
                pool.dma_start(sk, a["peer_sub_keys"][layer].rearrange("h s k d -> k (h s) d")).then_inc(q["sk_ld"], 16)
                for stream in range(2):
                    rows_to(shift2[:, stream, :], modd[layer, stream, 3 * D:4 * D], q["mbc_sh2"])
                n += 1
                phase_end(pool, n)
                for stream in range(2):
                    modulation_row(layer, stream, 5, 0, q["mbc_g2"])
                rows_to(lnbc[:, 0, :], a["ln2_g"][layer], q["lnbc2"])
                rows_to(lnbc[:, 1, :], a["ln2_b"][layer], q["lnbc2"])
                n += 1
                phase_end(pool, n)
                pu, pv = a["peer_u"], a["peer_v"]
                nblk = BLOCKS[layer]
                base = sum(BLOCKS[:layer])

                def gather(ring, slot, table, column, done):
                    pool.indirect_dma_start(ring[:, slot, :], None, table,
                                            bass.IndirectOffsetOnAxis(ap=idx[:, column:column + 1], axis=0)).then_inc(done[slot], 16)

                def hold(s, value):
                    pool.wait_ge(s, value)
                    pool.sem_inc(passed[0], 1)

                def u_rows(b, h, first=False):
                    hold(*q.at("g_idx", b * PH + h + 1))
                    for k in range(TOPK):
                        if not (first and k < UR):
                            hold(*q.at("g_ud", b * SLOTS + h * TOPK + k - UR + 1))
                        gather(uring, k % UR, pu, (h % PH) * TOPK + k, s_u)
                        yield

                def v_rows(b, h, first=False):
                    for k in range(TOPK):
                        if not (first and k < UR):
                            hold(*q.at("g_vd", b * SLOTS + h * TOPK + k - UR + 1))
                        gather(vring, k % UR, pv, h * TOPK + k, s_v)
                        yield

                def both(*streams):
                    streams = list(streams)
                    while streams:
                        for s in list(streams):
                            if next(s, "end") == "end":
                                streams.remove(s)

                def body(b, last, first=False):
                    for h in range(1, PH):
                        both(u_rows(b, h), v_rows(b, h - 1, first and h == 1))
                    if last:
                        both(v_rows(b, PH - 1))
                    else:
                        both(u_rows(b, PH), v_rows(b, PH - 1))

                both(u_rows(0, 0, True))
                body(0, False, True)
                with pool.Fori(1, nblk - 1) as b:
                    body(b, False)
                body(nblk - 1, True)
                n += 1
                phase_end(pool, n)
                n += 1
                phase_end(pool, n)

        @block.scalar
        def _(act):
            def copy(dst, src):
                return act.activation(dst, src, ACT.Copy)

            act.wait_ge(s_load0, 96)
            act.activation(cond[:, :, :], cond[:, :, :], ACT.Silu).then_inc(s_cond, 1)
            act.wait_ge(s_eps, 1)
            roots = [0]
            n = 0

            def root(layer, count, scale=1.0, src=None):
                roots[0] += 1
                act.wait_ge(*S[layer].at("stat", roots[0]))
                act.activation(sd[:, 0:count], mv[:, 0:count, 1] if src is None else src, ACT.Sqrt, bias=eps[:, 0:1],
                               scale=scale).then_inc(S[layer]["root"], 1)

            for layer in range(DEPTH):
                q = S[layer]
                nblk = BLOCKS[layer]
                roots[0] = 0
                n += 1
                phase_end(act, n)
                root(layer, NB)
                tiles = in_tiles(layer)

                def in_evac(i):
                    c, t = tiles[i]
                    act.wait_ge(*q.at("in_mm", i + 1))
                    copy(proj[:, t, c * INW:(c + 1) * INW], PS[:, 4 + i % 4, 0:INW]).then_inc(q["in_eva"], 1)

                chunk0 = [i for i, (c, t) in enumerate(tiles) if c == 0]
                chunk2 = [i for i, (c, t) in enumerate(tiles) if c == 2]
                for t in range(NB):
                    act.wait_ge(*q.at("in_tr", t + 1))
                    for j in range(2):
                        copy(hT[:, 4 * j:4 * j + 4, t * P:(t + 1) * P],
                             PS[:, 2 * (t % 2) + j, :].rearrange("p (k n) -> p k n", k=4)).then_inc(q["in_hev"], 1)
                    if t < len(chunk0):
                        in_evac(t)
                for i in range(len(chunk0), len(tiles)):
                    if in_owner(tiles[i]) == "act":
                        in_evac(i)
                    if i == chunk2[2]:
                        root(layer, NB * 10, 1.0 / HD, rstd[:, :])
                act.wait_ge(*q.at("lo_rt", 1))
                copy(cols[:, :], PS[:, 0, 0:GROUPS + 2 * (TAPS + 2)]).then_inc(q["lo_rev"], 1)
                act.wait_ge(q["in_eva"], sum(in_owner(x) == "act" for x in tiles))
                for t in range(nblk):
                    act.activation(proj[:, t, G_AT:G_AT + CW], proj[:, t, G_AT:G_AT + CW], ACT.Sigmoid).then_inc(q["lo_sig"], 1)
                for t in range(NB):
                    act.wait_ge(*q.at("at_tr", t + 1))
                    if t < nblk:
                        copy(qT[:, :, t * P:(t + 1) * P], PS[:, 2 * (t % 2), :].rearrange("p (j n) -> p j n", j=REP))
                    copy(kT[:, t * P:(t + 1) * P], PS[:, 2 * (t % 2) + 1, 0:P]).then_inc(q["at_qev"], 1)

                def place(t):
                    return PAD + t * P if t < NLAT else 3 * PAD + t * P

                for t in range(nblk):
                    act.wait_ge(*q.at("lo_gt", t + 1))
                    copy(cin[:, :, place(t):place(t) + P], PS[:, 4 + t % 2, 0:CW].rearrange("p (c n) -> p c n", c=2)).then_inc(q["lo_cin"], 1)
                n += 1
                phase_end(act, n)
                units = att_units(layer)

                def keys_of(first):
                    return range(NB) if first == 0 else range(NLAT, NB)

                def evac_probs(i):
                    first, m, h, t = units[i]
                    kb = len(keys_of(first))
                    if t == first and head_no(i) >= 2:
                        act.wait_ge(*q.at("at_pv", head_no(i) - 1))
                    act.wait_ge(*q.at("at_t", i + 1))
                    copy(probsT[:, head_no(i) % 2, :].rearrange("p (k n) -> p k n", k=NB)[:, 0:kb, (t - first) * P:(t - first + 1) * P],
                         PSf[:, 4 * 512:4 * 512 + kb * P].rearrange("p (k n) -> p k n", k=kb)).then_inc(q["at_tev"], 1)

                def head_no(i):
                    first, m, h, t = units[i]
                    return h if first == 0 else NQ + h

                def evac_out(i):
                    first, m, h, t = units[i]
                    pair = head_no(i) // 2
                    act.wait_ge(*q.at("at_pv", head_no(i) + 1))
                    copy(hT[:, h // 2, first * P:(first + m) * P], PS[:, 6 + pair % 2, 0:m * P]).then_inc(q["at_oev"], 1)

                def pair_end(i):
                    first, m, h, t = units[i]
                    return t == first + m - 1 and h % 2 == 1

                for i in range(len(units)):
                    first, m, h, t = units[i]
                    nk = len(keys_of(first)) * P
                    act.wait_ge(*q.at("at_max", i + 1))
                    if i >= 2:
                        act.wait_ge(*q.at("at_t", i - 1))
                    act.activation(probs[:, i % 2, 0:nk], PSf[:, (i % 2) * 1024:(i % 2) * 1024 + nk], ACT.Exp, bias=tiny[:, i % 4:i % 4 + 1],
                                   scale=SCALE, accum_out=tiny[:, 4 + i % 4:5 + i % 4]).then_inc(q["at_exp"], 1)
                    if i >= 1:
                        evac_probs(i - 1)
                    act.wait_ge(*q.at("at_rcp", i + 1))
                    act.activation(probs[:, i % 2, 0:nk], probs[:, i % 2, 0:nk], ACT.Copy, scale=tiny[:, 8 + i % 4:9 + i % 4]).then_inc(q["at_nrm"], 1)
                    if i >= 3 and pair_end(i - 3):
                        evac_out(i - 3)
                evac_probs(len(units) - 1)
                for i in range(len(units) - 3, len(units)):
                    if pair_end(i):
                        evac_out(i)
                n += 1
                phase_end(act, n)
                act.wait_ge(*q.at("lo_wt", 1))
                copy(wsT, PS[:, 0, :].rearrange("p (g n) -> p g n", g=GROUPS)).then_inc(q["lo_wev"], 1)
                for t in range(nblk):
                    act.activation(proj[:, t, U_AT:U_AT + 2 * GW], proj[:, t, U_AT:U_AT + 2 * GW], ACT.Gelu_apprx_tanh).then_inc(q["lo_gelu"], 1)
                root(layer, nblk)
                for t in range(nblk):
                    act.wait_ge(*q.at("lo_ct", t + 1))
                    copy(cy[:, t, :], PS[:, 2 + t % 2, 0:CW]).then_inc(q["lo_cy"], 1)
                root(layer, nblk)
                for t in range(nblk):
                    act.wait_ge(*q.at("lo_ygt", t + 1))
                    copy(hT[:, 4:6, t * P:(t + 1) * P], PS[:, t % 2, 0:CW].rearrange("p (k n) -> p k n", k=2)).then_inc(q["lo_yge"], 1)
                for t in range(nblk):
                    act.wait_ge(*q.at("lo_cn", t + 1))
                    act.activation(cy[:, t, :], cy[:, t, :], ACT.Silu).then_inc(q["lo_silu"], 1)
                for t in range(nblk):
                    act.wait_ge(*q.at("lo_st", t + 1))
                    copy(sT[:, :, t * P:(t + 1) * P], PS[:, t % 2, 0:CW].rearrange("p (k n) -> p k n", k=2)).then_inc(q["lo_se"], 1)
                for mo in range(2):
                    bias = cols[:, GROUPS + mo * (TAPS + 2) + TAPS + 1:GROUPS + mo * (TAPS + 2) + TAPS + 2]
                    for s, (t0, t1) in enumerate(((0, LAT), (LAT, TOK))[:1 + (nblk == NB)]):
                        act.wait_ge(*q.at("lo_pw", mo * (1 + (nblk == NB)) + s + 1))
                        act.activation(hT[:, 6 + mo, t0:t1], PS[:, 2 + 2 * mo + s, 0:t1 - t0], ACT.Identity, bias=bias).then_inc(q["lo_pwe"], 1)
                n += 1
                phase_end(act, n)
                for j in range(4):
                    act.wait_ge(*q.at("sk_tr", j + 1))
                    copy(skT[:, 4 * j:4 * j + 4, :], PS[:, 4 + j, :].rearrange("p (k n) -> p k n", k=4)).then_inc(q["sk_ev"], 1)

                def peer_input(t):
                    act.wait_ge(*q.at("ph_tr", t + 1))
                    for j in range(2):
                        copy(hT[:, 4 * j:4 * j + 4, t * P:(t + 1) * P],
                             PS[:, 4 + 2 * (t % 2) + j, :].rearrange("p (k n) -> p k n", k=4)).then_inc(q["ph_hev"], 1)

                for t in range(nblk):
                    root(layer, 1, 1.0, mv[:, t, 1:2])
                    root(layer, 1, 1.0, mv[:, t, 1:2])
                    if t >= 2:
                        peer_input(t - 2)
                peer_input(nblk - 2)
                peer_input(nblk - 1)
                n += 1
                phase_end(act, n)
                for hp in range(2 * PH):
                    act.wait_ge(*q.at("q_mm", hp + 1))
                    if hp >= 2:
                        act.wait_ge(*q.at("q_s", hp - 1))
                    copy(qs[:, hp % 2, 0:nblk * P], PSf[:, (hp % 2) * 1024:(hp % 2) * 1024 + nblk * P]).then_inc(q["q_ev"], 1)
                n += 1
                phase_end(act, n)

                def hold(s, value):
                    act.wait_ge(s, value)
                    act.sem_inc(passed[1], 1)

                def gates(b, h):
                    act.wait_ge(*q.at("g_best", b * PH + h + 1))
                    act.activation(gate[:, h * TOPK:(h + 1) * TOPK], gate[:, h * TOPK:(h + 1) * TOPK], ACT.Exp,
                                   accum_out=gsum[:, h:h + 1])

                def gelu(b, h):
                    act.wait_ge(*q.at("g_ud", b * SLOTS + (h + 1) * TOPK))
                    act.activation(gel[:, h * TOPK:(h + 1) * TOPK], actv[:, h * TOPK:(h + 1) * TOPK], ACT.Gelu_apprx_tanh).then_inc(q["g_gel"], 1)

                def diagonals(b, h, first=False):
                    act.wait_ge(*q.at("g_w", b * PH + h + 1))
                    for k in range(TOPK):
                        if not (first and k < 4):
                            act.wait_ge(*q.at("g_vd", b * SLOTS + h * TOPK + k - 3))
                        act.activation(dg[:, k % 4, :], ident[:, :], ACT.Copy, scale=wgt[:, h * TOPK + k:h * TOPK + k + 1]).then_inc(q["g_dg"], 1)

                def y_out(b):
                    act.wait_ge(*q.at("g_vd", (b + 1) * SLOTS))
                    act.sem_inc(passed[1], 1)
                    for j in range(2):
                        dst = H2f[:, bass.ds(b * D + j * 512, 512)] if not isinstance(b, int) else H2f[:, b * D + j * 512:b * D + j * 512 + 512]
                        copy(dst, PS[:, j, :]).then_inc(q["g_y"], 1)

                def body(b, last, first=False):
                    for h in range(1, PH + 1):
                        gelu(b, h - 1)
                        diagonals(b, h - 1, first and h == 1)
                        for ahead, hh in top_steps(first)[h]:
                            if ahead == 0 or not last:
                                gates(b + ahead, hh)
                    y_out(b)

                gates(0, 0)
                gates(0, 1)
                body(0, False, True)
                with act.Fori(1, nblk - 1) as b:
                    body(b, False)
                body(nblk - 1, True)
                n += 1
                phase_end(act, n)
                root(layer, nblk)
                n += 1
                phase_end(act, n)

        @block.tensor
        def _(pe):
            wcount = [0]

            def weights(layer, kind, i):
                n = chunk_number(layer, kind, i)
                pe.wait_ge(s_wfull[n % 2], 16 * (n // 2 + 1))
                return wv[n % 2]

            pe.wait_ge(s_const, 2)
            pe.wait_ge(s_cond, 1)
            n = 0
            for layer in range(DEPTH):
                q = S[layer]
                nblk = BLOCKS[layer]
                for i in range(MODC):
                    w = weights(layer, "mod", i)
                    if i >= 2:
                        pe.wait_ge(*q.at("mod_ev", i - 1))
                    for k in range(KD):
                        mm = pe.matmul(PS[0:2, i % 2, :], cond[:, :, k], w[:, k, :], start=(k == 0), stop=(k == KD - 1))
                    mm.then_inc(q["mod_mm"], 1)
                n += 1
                phase_end(pe, n)
                tiles = in_tiles(layer)

                def in_mm(i):
                    c, t = tiles[i]
                    w = weights(layer, "in", c)
                    if i >= 4:
                        j = i - 4
                        owner = in_owner(tiles[j])
                        pe.wait_ge(q["in_eva" if owner == "act" else "in_evd"], sum(in_owner(x) == owner for x in tiles[:j + 1]))
                    for k in range(KD):
                        mm = pe.matmul(PS[:, 4 + i % 4, 0:INW], hT[:, k, t * P:(t + 1) * P], w[:, k, 0:INW], start=(k == 0), stop=(k == KD - 1))
                    mm.then_inc(q["in_mm"], 1)

                chunk0 = [i for i, (c, t) in enumerate(tiles) if c == 0]
                for t in range(NB):
                    pe.wait_ge(*q.at("in_h", t + 1))
                    if t >= 2:
                        pe.wait_ge(*q.at("in_hev", 2 * (t - 1)))
                    for k in range(KD):
                        tr = pe.transpose(PS[:, 2 * (t % 2) + k // 4, (k % 4) * P:(k % 4 + 1) * P], hb[:, t % 2, k * P:(k + 1) * P], ident[:, :])
                    tr.then_inc(q["in_tr"], 1)
                    pe.wait_ge(*q.at("in_hev", 2 * (t + 1)))
                    if t < len(chunk0):
                        in_mm(t)
                for i in range(len(chunk0), len(tiles)):
                    in_mm(i)
                pe.wait_ge(*q.at("row_ld", 64))
                pe.transpose(PS[:, 0, 0:GROUPS], bsr[0:GROUPS, :], ident[0:GROUPS, 0:GROUPS])
                for c in range(2):
                    tr = pe.transpose(PS[:, 0, GROUPS + c * (TAPS + 2):GROUPS + (c + 1) * (TAPS + 2)], rows[0:TAPS + 2, c * P:(c + 1) * P],
                                      ident[0:TAPS + 2, 0:TAPS + 2])
                tr.then_inc(q["lo_rt"], 1)
                pe.wait_ge(*q.at("lo_rev", 1))
                for t in range(NB):
                    pe.wait_ge(*q.at("at_q", t + 1))
                    if t >= 2:
                        pe.wait_ge(*q.at("at_qev", t - 1))
                    src = qr[:, t, :]
                    if t < nblk:
                        for j in range(REP):
                            pe.transpose(PS[:, 2 * (t % 2), j * P:(j + 1) * P], src[:, j * P:(j + 1) * P], ident[:, :])
                    pe.transpose(PS[:, 2 * (t % 2) + 1, 0:P], src[:, AW:AW + KW], ident[:, :]).then_inc(q["at_tr"], 1)
                pe.wait_ge(q["in_eva"], sum(in_owner(x) == "act" for x in tiles))
                for t in range(nblk):
                    pe.wait_ge(*q.at("lo_glu", t + 1))
                    if t >= 2:
                        pe.wait_ge(*q.at("lo_cin", t - 1))
                    for c in range(2):
                        tr = pe.transpose(PS[:, 4 + t % 2, c * P:(c + 1) * P], proj[:, t, A_AT + c * P:A_AT + (c + 1) * P], ident[:, :])
                    tr.then_inc(q["lo_gt"], 1)
                n += 1
                phase_end(pe, n)
                units = att_units(layer)

                def keys_of(first):
                    return range(NB) if first == 0 else range(NLAT, NB)

                def scores(i):
                    first, m, h, t = units[i]
                    g, j = h // REP, h % REP
                    if i >= 2:
                        pe.wait_ge(*q.at("at_exp", i - 1))
                    k0, k1 = keys_of(first)[0] * P, (keys_of(first)[-1] + 1) * P
                    for part, at in enumerate(range(k0, k1, 512)):
                        end = min(at + 512, k1)
                        mm = pe.matmul(PS[:, 2 * (i % 2) + part, 0:end - at], qT[g * HD:(g + 1) * HD, j, t * P:(t + 1) * P],
                                       kT[g * HD:(g + 1) * HD, at:end], start=True, stop=True)
                    mm.then_inc(q["at_s"], 1)

                def turn(i):
                    first, m, h, t = units[i]
                    pe.wait_ge(*q.at("at_nrm", i + 1))
                    if i >= 1:
                        pe.wait_ge(*q.at("at_tev", i))
                    for k in range(len(keys_of(first))):
                        tr = pe.transpose(PSf[:, 4 * 512 + k * P:4 * 512 + (k + 1) * P], probs[:, i % 2, k * P:(k + 1) * P], ident[:, :])
                    tr.then_inc(q["at_t"], 1)

                def head_end(i):
                    first, m, h, t = units[i]
                    return t == first + m - 1

                def values(i):
                    first, m, h, t = units[i]
                    g = h // REP
                    no = h if first == 0 else NQ + h
                    pair = no // 2
                    pe.wait_ge(*q.at("at_tev", i + 1))
                    if pair >= 2 and no % 2 == 0:
                        pe.wait_ge(*q.at("at_oev", pair - 1))
                    kbs = list(keys_of(first))
                    for k, kb in enumerate(kbs):
                        mm = pe.matmul(PS[(h % 2) * HD:(h % 2 + 1) * HD, 6 + pair % 2, 0:m * P],
                                       proj[:, kb, AW + KW + g * HD:AW + KW + (g + 1) * HD],
                                       probsT[:, no % 2, :].rearrange("p (k n) -> p k n", k=NB)[:, k, 0:m * P],
                                       start=(k == 0), stop=(k == len(kbs) - 1), skip_group_check=True)
                    mm.then_inc(q["at_pv"], 1)

                scores(0)
                scores(1)
                for i in range(len(units)):
                    if i + 2 < len(units):
                        scores(i + 2)
                    turn(i)
                    if i >= 1 and head_end(i - 1):
                        values(i - 1)
                values(len(units) - 1)
                n += 1
                phase_end(pe, n)
                pe.wait_ge(*q.at("lo_ld", 96))
                for g in range(GROUPS):
                    tr = pe.transpose(PS[:, 0, g * P:(g + 1) * P], ws[:, g, :], ident[:, :])
                tr.then_inc(q["lo_wt"], 1)
                pe.wait_ge(*q.at("lo_wev", 1))
                for t in range(nblk):
                    pe.wait_ge(*q.at("lo_vn", t + 1))
                    for g in range(GROUPS):
                        mm = pe.matmul(PS[:, 4 + t // 2, (t % 2) * GW + g * GC:(t % 2) * GW + (g + 1) * GC], wsT[:, g, :],
                                       proj[:, t, V_AT + g * GC:V_AT + (g + 1) * GC], start=True, stop=True)
                    mm.then_inc(q["lo_gm"], 1)
                streams = 1 + (nblk == NB)
                pe.wait_ge(*q.at("lo_tap", TAPS * 2 * streams))
                for t in range(nblk):
                    if t >= 2:
                        pe.wait_ge(*q.at("lo_cy", t - 1))
                    for c in range(2):
                        tr = pe.transpose(PS[:, 2 + t % 2, c * P:(c + 1) * P], cacc[:, c, t * P:(t + 1) * P], ident[:, :])
                    tr.then_inc(q["lo_ct"], 1)
                for t in range(nblk):
                    pe.wait_ge(*q.at("lo_yg", t + 1))
                    if t >= 2:
                        pe.wait_ge(*q.at("lo_yge", t - 1))
                    for c in range(2):
                        tr = pe.transpose(PS[:, t % 2, c * P:(c + 1) * P], proj[:, t, U_AT + c * P:U_AT + (c + 1) * P], ident[:, :])
                    tr.then_inc(q["lo_ygt"], 1)
                pe.wait_ge(*q.at("lo_yge", nblk))
                for t in range(nblk):
                    pe.wait_ge(*q.at("lo_silu", t + 1))
                    if t >= 2:
                        pe.wait_ge(*q.at("lo_se", t - 1))
                    for c in range(2):
                        tr = pe.transpose(PS[:, t % 2, c * P:(c + 1) * P], cy[:, t, c * P:(c + 1) * P], ident[:, :])
                    tr.then_inc(q["lo_st"], 1)
                pe.wait_ge(*q.at("lo_se", nblk))
                for mo in range(2):
                    for s, (t0, t1) in enumerate(((0, LAT), (LAT, TOK))[:streams]):
                        for k in range(2):
                            mm = pe.matmul(PS[:, 2 + 2 * mo + s, 0:t1 - t0], wpw[:, k, mo * P:(mo + 1) * P], sT[:, k, t0:t1], start=(k == 0), stop=(k == 1))
                        mm.then_inc(q["lo_pw"], 1)
                n += 1
                phase_end(pe, n)
                wo = [weights(layer, "out", c) for c in range(OUTC)]

                def peer_input(t):
                    pe.wait_ge(*q.at("ph_h", t + 1))
                    if t >= 2:
                        pe.wait_ge(*q.at("ph_hev", 2 * (t - 1)))
                    for k in range(KD):
                        tr = pe.transpose(PS[:, 4 + 2 * (t % 2) + k // 4, (k % 4) * P:(k % 4 + 1) * P], H2[:, t, k * P:(k + 1) * P], ident[:, :])
                    tr.then_inc(q["ph_tr"], 1)

                for t in range(nblk):
                    for c in range(OUTC):
                        i = t * OUTC + c
                        if i >= 4:
                            pe.wait_ge(*q.at("ou_ev", i - 3))
                        for k in range(KD):
                            mm = pe.matmul(PS[:, i % 4, :], hT[:, k, t * P:(t + 1) * P], wo[c][:, k, :], start=(k == 0), stop=(k == KD - 1))
                        mm.then_inc(q["ou_mm"], 1)
                    if t == 0:
                        pe.wait_ge(*q.at("sk_ld", 16))
                        for hp in range(2 * PH):
                            tr = pe.transpose(PS[:, 4 + hp // 4, (hp % 4) * P:(hp % 4 + 1) * P], sk[:, hp, :], ident[:, :])
                            if hp % 4 == 3:
                                tr.then_inc(q["sk_tr"], 1)
                    if t == 1:
                        pe.wait_ge(*q.at("sk_ev", 4))
                    if t >= 2:
                        peer_input(t - 2)
                peer_input(nblk - 2)
                peer_input(nblk - 1)
                n += 1
                phase_end(pe, n)
                def queries(hp):
                    w = weights(layer, "q", hp // 4)
                    if hp >= 2:
                        pe.wait_ge(*q.at("q_ev", hp - 1))
                    for s, (t0, t1) in enumerate(((0, LAT), (LAT, TOK))[:streams]):
                        for k in range(KD):
                            mm = pe.matmul(PS[:, 2 * (hp % 2) + s, 0:t1 - t0], w[:, k, (hp % 4) * P:(hp % 4 + 1) * P], hT[:, k, t0:t1],
                                           start=(k == 0), stop=(k == KD - 1))
                    mm.then_inc(q["q_mm"], 1)

                def key_scores(hp):
                    pe.wait_ge(*q.at("q_ev", hp + 1))
                    if hp >= 2:
                        pe.wait_ge(*q.at("q_tk", nblk * (hp - 1)))
                    for t in range(nblk):
                        at = 4 * 512 + (hp % 2) * 1024 + t * P
                        mm = pe.matmul(PSf[:, at:at + P], qs[:, hp % 2, t * P:(t + 1) * P], skT[:, hp, :], start=True, stop=True)
                    mm.then_inc(q["q_s"], 1)

                queries(0)
                for hp in range(2 * PH):
                    if hp + 1 < 2 * PH:
                        queries(hp + 1)
                    key_scores(hp)
                n += 1
                phase_end(pe, n)
                base = sum(BLOCKS[:layer])

                def head(b, h):
                    for k in range(TOPK):
                        pe.wait_ge(s_v[k % UR], 16 * ((base + b) * SLOTS // UR + h * TOPK // UR + k // UR + 1))
                        pe.wait_ge(*q.at("g_dg", b * SLOTS + h * TOPK + k + 1))
                        for j in range(2):
                            mm = pe.matmul(PS[:, j, :], dg[:, k % 4, :], vring[:, k % UR, j * 512:(j + 1) * 512],
                                           start=(h == 0 and k == 0), stop=(h == PH - 1 and k == TOPK - 1), skip_group_check=True)
                        mm.then_inc(q["g_vd"], 1)

                def body(b, first=False):
                    if not first:
                        pe.wait_ge(*q.at("g_y", 2 * b))
                    for h in range(PH):
                        head(b, h)

                body(0, True)
                with pe.Fori(1, nblk - 1) as b:
                    body(b)
                body(nblk - 1)
                n += 1
                phase_end(pe, n)
                n += 1
                phase_end(pe, n)

        @block.vector
        def _(dve):
            ch = Chain(dve, c_dve)
            dve.memset(eps[:, :], EPS).then_inc(s_eps, 1)
            dve.wait_ge(s_const, 2)
            dve.wait_ge(s_load0, 96)
            n = 0
            roots = [0]

            def statistics(layer, t, src):
                width = src.shape[-1]
                parts = max(1, width // 512)
                for j in range(parts):
                    ch(dve.bn_stats(st[:, t, j, :], src[:, j * 512:min(width, (j + 1) * 512)]))
                ch(dve.bn_aggr(mv[:, t, :], st[:, t, 0:parts, :]))

            def inverse_roots(layer, count, mark):
                ch(mark)
                roots[0] += 1
                dve.wait_ge(*S[layer].at("root", roots[0]))
                ch(dve.reciprocal(rstd[:, 0:count], sd[:, 0:count]))

            def normalise(dst, src, t):
                return dve.tensor_scalar(dst, src, mv[:, t, 0:1], rstd[:, t:t + 1], ALU.subtract, ALU.mult)

            def all_statistics(layer, count, source):
                for t in range(count):
                    statistics(layer, t, source(t))
                ch.sig(dve.tensor_copy(tiny[:, 12:13], mv[:, count - 1, 1:2]), S[layer]["stat"])
                roots[0] += 1
                dve.wait_ge(*S[layer].at("root", roots[0]))
                ch(dve.reciprocal(rstd[:, 0:count], sd[:, 0:count]))

            for layer in range(DEPTH):
                q = S[layer]
                nblk = BLOCKS[layer]
                roots[0] = 0
                dve.wait_ge(*q.at("bmod", 16))
                for i in range(MODC):
                    dve.wait_ge(*q.at("mod_mm", i + 1))
                    dve.tensor_tensor(modrow[0:2, i * 512:(i + 1) * 512], PS[0:2, i % 2, :], bmod[0:2, i * 512:(i + 1) * 512], ALU.add).then_inc(q["mod_ev"], 1)
                n += 1
                phase_end(dve, n)
                all_statistics(layer, NB, lambda t: X[:, t, :])
                dve.wait_ge(*q.at("mbc_in", 64))
                for t in range(NB):
                    s = int(t >= NLAT)
                    if t >= 2:
                        dve.wait_ge(*q.at("in_tr", t - 1))
                    ch(normalise(hb[:, t % 2, :], X[:, t, :], t))
                    ch(dve.scalar_tensor_tensor(hb[:, t % 2, :], modbc[:, s, 1, :], 1.0, hb[:, t % 2, :], ALU.add, ALU.mult))
                    dve.tensor_tensor(hb[:, t % 2, :], hb[:, t % 2, :], modbc[:, s, 0, :], ALU.add).then_inc(q["in_h"], 1)
                tiles = in_tiles(layer)
                for i, (c, t) in enumerate(tiles):
                    if in_owner((c, t)) == "dve":
                        dve.wait_ge(*q.at("in_mm", i + 1))
                        ch.sig(dve.tensor_copy(proj[:, t, c * INW:(c + 1) * INW], PS[:, 4 + i % 4, 0:INW]), q["in_evd"])
                dve.wait_ge(q["in_eva"], sum(in_owner(x) == "act" and x[0] < 2 for x in tiles))
                ch(dve.memset(cin, 0.0))
                ch(dve.memset(rstd[:, :], 1.0))
                for t in range(NB):
                    h0 = 0 if t < nblk else NQ
                    w = (NQ + NKV - h0) * HD
                    src = proj[:, t, h0 * HD:(NQ + NKV) * HD]
                    flat = qn.rearrange("p h d -> p (h d)")[:, 0:w]
                    ch(dve.tensor_tensor(flat, src, src, ALU.mult))
                    ch(dve.tensor_reduce(rstd[:, t * 10 + h0:t * 10 + 10], flat.rearrange("p (h d) -> p h d", d=HD), AX_X, ALU.add))
                ch.sig(dve.tensor_copy(tiny[:, 12:13], rstd[:, 0:1]), q["stat"])
                roots[0] += 1
                dve.wait_ge(*q.at("root", roots[0]))
                ch(dve.reciprocal(rstd[:, :], sd[:, :]))
                dve.wait_ge(*q.at("gqk", 32))
                for t in range(NB):
                    h0 = 0 if t < nblk else NQ
                    src = proj[:, t, h0 * HD:(NQ + NKV) * HD].rearrange("p (h d) -> p h d", d=HD)
                    dst = qr[:, t, :].rearrange("p (h d) -> p h d", d=HD)[:, h0:NQ + NKV, :]
                    if h0 == 0:
                        ch(dve.tensor_tensor(qn[:, 0:NQ, :].rearrange("p (j g) d -> p g j d", g=NKV),
                                             src[:, 0:NQ, :].rearrange("p (g j) d -> p g j d", g=NKV),
                                             rstd[:, t * 10:t * 10 + NQ].rearrange("p (g j) -> p g j", g=NKV).unsqueeze(3).to_broadcast([P, NKV, REP, HD]),
                                             ALU.mult))
                    ch(dve.tensor_tensor(qn[:, NQ:NQ + NKV, :], src[:, NQ - h0:NQ + NKV - h0, :],
                                         rstd[:, t * 10 + NQ:t * 10 + 10].unsqueeze(2).to_broadcast([P, NKV, HD]), ALU.mult))
                    if t >= NLAT:
                        ch.sig(dve.tensor_tensor(dst, qn[:, h0:NQ + NKV, :], gqk[:, h0:NQ + NKV, :], ALU.mult), q["at_q"])
                        continue
                    ch(dve.tensor_tensor(qn, qn, gqk, ALU.mult))
                    halves = qn.rearrange("p h (a s f) -> p h a s f", a=2, s=2)
                    rotated = qr[:, t, :].rearrange("p (h a s f) -> p h a s f", h=NQ + NKV, a=2, s=2)
                    x1, x2 = halves[:, :, :, 0, :], halves[:, :, :, 1, :]
                    cs = cosT[:, t, :, :].unsqueeze(1).to_broadcast([P, NQ + NKV, 2, 16])
                    sn = sinT[:, t, :, :].unsqueeze(1).to_broadcast([P, NQ + NKV, 2, 16])
                    va = tA.rearrange("p (h a f) -> p h a f", h=NQ + NKV, a=2)
                    vb = tB.rearrange("p (h a f) -> p h a f", h=NQ + NKV, a=2)
                    ch(dve.tensor_tensor(va, x1, cs, ALU.mult))
                    ch(dve.tensor_tensor(vb, x2, sn, ALU.mult))
                    ch(dve.tensor_tensor(rotated[:, :, :, 0, :], va, vb, ALU.subtract))
                    ch(dve.tensor_tensor(va, x1, sn, ALU.mult))
                    ch(dve.tensor_tensor(vb, x2, cs, ALU.mult))
                    ch.sig(dve.tensor_tensor(rotated[:, :, :, 1, :], va, vb, ALU.add), q["at_q"])
                for t in range(nblk):
                    dve.wait_ge(*q.at("lo_sig", t + 1))
                    dve.tensor_tensor(proj[:, t, A_AT:A_AT + CW], proj[:, t, A_AT:A_AT + CW], proj[:, t, G_AT:G_AT + CW], ALU.mult).then_inc(q["lo_glu"], 1)
                n += 1
                phase_end(dve, n)
                units = att_units(layer)

                def maximum(i):
                    nk = (NB if units[i][0] == 0 else NCTX) * P
                    dve.wait_ge(*q.at("at_s", i + 1))
                    if i >= 4:
                        dve.wait_ge(*q.at("at_exp", i - 3))
                    ch(dve.tensor_reduce(tiny[:, 13:14], PSf[:, (i % 2) * 1024:(i % 2) * 1024 + nk], AX_X, ALU.max))
                    ch.sig(dve.tensor_scalar(tiny[:, i % 4:i % 4 + 1], tiny[:, 13:14], -SCALE, None, ALU.mult), q["at_max"])

                def reciprocal(i):
                    dve.wait_ge(*q.at("at_exp", i + 1))
                    ch.sig(dve.reciprocal(tiny[:, 8 + i % 4:9 + i % 4], tiny[:, 4 + i % 4:5 + i % 4]), q["at_rcp"])

                turns = [(c, s) for c in range(2) for s in range(1 + (nblk == NB))]

                def taps():
                    for tap in range(TAPS):
                        for j, (c, s) in enumerate(turns):
                            t0, t1 = ((0, LAT), (LAT, TOK))[s]
                            src = cin[:, c, 2 * PAD * s + t0 + tap:2 * PAD * s + t1 + tap]
                            acc = cacc[:, c, t0:t1]
                            at = GROUPS + c * (TAPS + 2)
                            wcol = cols[:, at + tap:at + tap + 1]
                            if tap == 0:
                                dve.tensor_scalar(acc, src, wcol, cols[:, at + TAPS:at + TAPS + 1], ALU.mult, ALU.add).then_inc(q["lo_tap"], 1)
                            else:
                                dve.wait_ge(*q.at("lo_tap", (tap - 1) * len(turns) + j + 1))
                                dve.scalar_tensor_tensor(acc, src, wcol, acc, ALU.mult, ALU.add).then_inc(q["lo_tap"], 1)
                            yield

                tap = taps()
                maximum(0)
                for i in range(len(units)):
                    if i + 1 < len(units):
                        maximum(i + 1)
                    next(tap, None)
                    reciprocal(i)
                    next(tap, None)
                    if nblk == NB:
                        next(tap, None)
                for _ in tap:
                    pass
                n += 1
                phase_end(dve, n)
                dve.wait_ge(*q.at("lo_ld", 96))
                dve.wait_ge(*q.at("lo_gelu", nblk))
                all_statistics(layer, nblk, lambda t: proj[:, t, V_AT:V_AT + GW])
                for t in range(nblk):
                    v = proj[:, t, V_AT:V_AT + GW]
                    ch(normalise(v, v, t))
                    ch(dve.tensor_tensor(v, v, gln[:, 0, :], ALU.mult))
                    ch.sig(dve.tensor_tensor(v, v, gln[:, 1, :], ALU.add), q["lo_vn"])
                dve.wait_ge(*q.at("lo_gm", nblk))
                for t in range(nblk):
                    for g in range(GROUPS):
                        u = proj[:, t, U_AT + g * GC:U_AT + (g + 1) * GC]
                        ins = dve.scalar_tensor_tensor(u, PS[:, 4 + t // 2, (t % 2) * GW + g * GC:(t % 2) * GW + (g + 1) * GC], cols[:, g:g + 1], u, ALU.add, ALU.mult)
                        if g < GROUPS - 1:
                            ch(ins)
                    ch.sig(ins, q["lo_yg"])
                dve.wait_ge(*q.at("lo_cy", nblk))
                all_statistics(layer, nblk, lambda t: cy[:, t, :])
                for t in range(nblk):
                    ch(normalise(cy[:, t, :], cy[:, t, :], t))
                    ch(dve.tensor_tensor(cy[:, t, :], cy[:, t, :], cln[:, 0, :], ALU.mult))
                    ch.sig(dve.tensor_tensor(cy[:, t, :], cy[:, t, :], cln[:, 1, :], ALU.add), q["lo_cn"])
                n += 1
                phase_end(dve, n)
                dve.wait_ge(*q.at("mbc_out", 32))
                dve.wait_ge(*q.at("lnbc", 32))
                dve.wait_ge(*q.at("mbc_sc2", 32))
                dve.wait_ge(*q.at("mbc_sh2", 32))

                def block_statistics(t):
                    for j in range(2):
                        dve.bn_stats(st[:, t, j, :], X[:, t, j * 512:(j + 1) * 512]).then_inc(c_dve, 1)
                        ch.n += 1
                    dve.wait_ge(c_dve, ch.n)
                    ch.sig(dve.bn_aggr(mv[:, t, :], st[:, t, :, :]), S[layer]["stat"])
                    roots[0] += 1
                    dve.wait_ge(S[layer]["root"], roots[0])
                    ch(dve.reciprocal(rstd[:, t:t + 1], sd[:, 0:1]))

                for t in range(nblk):
                    s = int(t >= NLAT)
                    for c in range(OUTC):
                        i = t * OUTC + c
                        dve.wait_ge(*q.at("ou_mm", i + 1))
                        cs = slice(c * 512, (c + 1) * 512)
                        ch.sig(dve.tensor_tensor(spare[:, c, :], PS[:, i % 4, :], modbc[:, s, 0, cs], ALU.mult), q["ou_ev"])
                        ch(dve.scalar_tensor_tensor(X[:, t, cs], X[:, t, cs], ALPHA, spare[:, c, :], ALU.mult, ALU.add))
                    block_statistics(t)
                    ch(normalise(X[:, t, :], X[:, t, :], t))
                    ch(dve.tensor_tensor(X[:, t, :], X[:, t, :], lnbc[:, 0, :], ALU.mult))
                    ch(dve.tensor_tensor(X[:, t, :], X[:, t, :], lnbc[:, 1, :], ALU.add))
                    block_statistics(t)
                    ch(normalise(H2[:, t, :], X[:, t, :], t))
                    ch(dve.scalar_tensor_tensor(H2[:, t, :], modbc[:, s, 1, :], 1.0, H2[:, t, :], ALU.add, ALU.mult))
                    ch.sig(dve.tensor_tensor(H2[:, t, :], H2[:, t, :], shift2[:, s, :], ALU.add), q["ph_h"])

                def layer_norm():
                    all_statistics(layer, nblk, lambda t: X[:, t, :])
                    for t in range(nblk):
                        ch(normalise(X[:, t, :], X[:, t, :], t))
                        ch(dve.tensor_tensor(X[:, t, :], X[:, t, :], lnbc[:, 0, :], ALU.mult))
                        ch(dve.tensor_tensor(X[:, t, :], X[:, t, :], lnbc[:, 1, :], ALU.add))

                n += 1
                phase_end(dve, n)
                for hp in range(2 * PH):
                    dve.wait_ge(*q.at("q_s", hp + 1))
                    for t in range(nblk):
                        at = 4 * 512 + (hp % 2) * 1024 + t * P
                        s = PSf[:, at:at + P]
                        v = V16[:, t, hp * TOPK:(hp + 1) * TOPK]
                        ix = I16[:, t, hp * TOPK:(hp + 1) * TOPK]
                        ch(dve.max(v[:, 0:8], s))
                        ch(dve.max_index(ix[:, 0:8], v[:, 0:8], s))
                        ch(dve.match_replace(scr, v[:, 0:8], s, LOWEST))
                        ch(dve.max(v[:, 8:16], scr))
                        ch.sig(dve.max_index(ix[:, 8:16], v[:, 8:16], scr), q["q_tk"])
                n += 1
                phase_end(dve, n)
                base = sum(BLOCKS[:layer])
                STEPS = 15

                def hold(s, value):
                    dve.wait_ge(s, value)
                    dve.sem_inc(s_hold, 1)

                def at(view, b, off, size):
                    if isinstance(b, int):
                        return view[:, b * (view.shape[-1] // NB) + off:b * (view.shape[-1] // NB) + off + size]
                    return view[:, bass.ds(b * (view.shape[-1] // NB) + off, size)]

                def best_experts(b, h):
                    done = [0]
                    origin = (b * PH + h + base * PH) * STEPS

                    def link(ins, apart=False):
                        ins.then_inc(c_tk, 1)
                        done[0] += 1
                        (hold if apart else dve.wait_ge)(c_tk, origin + done[0])

                    v = at(V16f, b, 2 * h * TOPK, 2 * TOPK)
                    ix = at(I16f, b, 2 * h * TOPK, 2 * TOPK)
                    c2 = cand.rearrange("p (i j) -> p i j", i=TOPK)
                    e2 = eq.rearrange("p (i j) -> p i j", i=TOPK)
                    k0 = h * TOPK
                    bst = best[:, k0:k0 + TOPK]

                    def down(x):
                        return x.unsqueeze(2).to_broadcast([P, TOPK, TOPK])

                    def across(x):
                        return x.unsqueeze(1).to_broadcast([P, TOPK, TOPK])

                    link(dve.tensor_tensor(c2, down(v[:, 0:TOPK]), across(v[:, TOPK:2 * TOPK]), ALU.add), True)
                    link(dve.max(bst[:, 0:8], cand), True)
                    link(dve.max_index(pos[:, 0:8], bst[:, 0:8], cand), True)
                    link(dve.match_replace(cand, bst[:, 0:8], cand, LOWEST), True)
                    link(dve.max(bst[:, 8:16], cand), True)
                    link(dve.max_index(pos[:, 8:16], bst[:, 8:16], cand))
                    gt = gate[:, k0:k0 + TOPK]
                    dve.tensor_scalar(gt, bst, bst[:, 0:1], None, ALU.subtract).then_inc(q["g_best"], 1)
                    link(dve.tensor_scalar(hilo[:, 0:TOPK], pos, 4, None, ALU.logical_shift_right))
                    link(dve.tensor_scalar(hilo[:, TOPK:2 * TOPK], pos, TOPK - 1, None, ALU.bitwise_and))
                    for half in range(2):
                        link(dve.tensor_tensor(e2, down(hilo[:, half * TOPK:(half + 1) * TOPK]), across(iota16[:, :]), ALU.is_equal), True)
                        link(dve.tensor_tensor(e2, e2, across(ix[:, half * TOPK:(half + 1) * TOPK]), ALU.mult))
                        link(dve.tensor_reduce(e12[:, half * TOPK:(half + 1) * TOPK], e2, AX_X, ALU.add))
                    link(dve.tensor_scalar(e12[:, 0:TOPK], e12[:, 0:TOPK], float(NK), float(layer * NEXP), ALU.mult, ALU.add))
                    dve.tensor_tensor(idx[:, k0:k0 + TOPK], e12[:, 0:TOPK], e12[:, TOPK:2 * TOPK], ALU.add).then_inc(q["g_idx"], 1)
                    assert done[0] == STEPS, done[0]

                def products(b, h, lo=0, hi=TOPK):
                    for k in range(lo, hi):
                        dve.wait_ge(s_u[k % UR], 16 * ((base + b) * SLOTS // UR + h * TOPK // UR + k // UR + 1))
                        col = (h % PH) * TOPK + k
                        dve.tensor_tensor_reduce(uring[:, k % UR, :], uring[:, k % UR, :], hcur, 1.0, 0.0, ALU.mult, ALU.add,
                                                 actv[:, col:col + 1]).then_inc(q["g_ud"], 1)

                def weigh(b, h):
                    dve.wait_ge(*q.at("g_gel", b * PH + h + 1))
                    dve.reciprocal(tiny[:, 9:10], gsum[:, h:h + 1]).then_inc(c_up, 1)
                    dve.wait_ge(c_up, (base + b) * PH + h + 1)
                    dve.scalar_tensor_tensor(wgt[:, h * TOPK:(h + 1) * TOPK], gel[:, h * TOPK:(h + 1) * TOPK], tiny[:, 9:10],
                                             gate[:, h * TOPK:(h + 1) * TOPK], ALU.mult, ALU.mult).then_inc(q["g_w"], 1)

                def current(b):
                    hold(*q.at("g_ud", b * SLOTS))
                    dve.tensor_copy(hcur, at(H2f, b, 0, D)).then_inc(q["g_h"], 1)
                    dve.wait_ge(*q.at("g_h", b + 1))

                def body(b, last, first=False):
                    for h in range(1, PH + 1):
                        tops = [(b + ahead, hh) for ahead, hh in top_steps(first)[h] if ahead == 0 or not last]
                        if h == PH and not last:
                            current(b + 1)
                        if h < PH or not last:
                            products(b, h, 0, 4)
                        weigh(b, h - 1)
                        if h < PH or not last:
                            products(b, h, 4, 10)
                        for top in tops[:1]:
                            best_experts(*top)
                        if h < PH or not last:
                            products(b, h, 10, TOPK)
                        for top in tops[1:]:
                            best_experts(*top)

                best_experts(0, 0)
                current(0)
                products(0, 0)
                best_experts(0, 1)
                body(0, False, True)
                with dve.Fori(1, nblk - 1) as b:
                    body(b, False)
                body(nblk - 1, True)
                n += 1
                phase_end(dve, n)
                dve.wait_ge(*q.at("mbc_g2", 32))
                dve.wait_ge(*q.at("lnbc2", 32))
                for t in range(nblk):
                    s = int(t >= NLAT)
                    ch(dve.tensor_tensor(H2[:, t, :], H2[:, t, :], modbc[:, s, 0, :], ALU.mult))
                    ch(dve.scalar_tensor_tensor(X[:, t, :], X[:, t, :], ALPHA, H2[:, t, :], ALU.mult, ALU.add))
                layer_norm()
                dve.tensor_copy(tiny[:, 12:13], tiny[:, 13:14]).then_inc(q["ep"], 1)
                n += 1
                phase_end(dve, n)


_INS = ['x', 'c', 'ctx', 'c_ctx', 'w_mod', 'b_mod', 'w_in', 'q_norm_g', 'k_norm_g', 'gmlp_ln_g', 'gmlp_ln_b', 'gmlp_w_s', 'gmlp_b_s',
        'conv_w_dw', 'conv_b_dw', 'conv_ln_g', 'conv_ln_b', 'conv_w_pw', 'conv_b_pw', 'w_out', 'ln1_g', 'ln1_b', 'ln2_g', 'ln2_b',
        'peer_w_q', 'peer_sub_keys', 'peer_u', 'peer_v']


def rope_tables():
    import numpy as np
    grid = 64
    half = HD // 4
    freqs = (np.float32(10000.0) ** (-np.arange(half, dtype=np.float32) / np.float32(half))).astype(np.float32)
    where = np.arange(LAT)
    angles = np.stack([(where // grid).astype(np.float32)[:, None] * freqs, (where % grid).astype(np.float32)[:, None] * freqs], 1)
    angles = angles.reshape(LAT, 2 * half).astype(np.float64)
    return np.cos(angles).astype(np.float32), np.sin(angles).astype(np.float32)


def kernel(**inputs):
    import numpy as _np
    import concourse.bacc as _bacc
    from concourse import mybir as _mybir
    from concourse.bass_utils import run_bass_kernel_spmd as _run

    nc = _bacc.Bacc("TRN2", target_bir_lowering=False, num_devices=1)
    arrays, aps = {}, {}
    shaped = {name: inputs[name] for name in _INS}
    for name in ("peer_u", "peer_v"):
        shaped[name] = inputs[name].reshape(DEPTH * NEXP, D)
    shaped["rope_cos"], shaped["rope_sin"] = rope_tables()
    for name, value in shaped.items():
        array = _np.ascontiguousarray(value)
        arrays[f"in_{name}_dram"] = array
        aps[name] = nc.dram_tensor(f"in_{name}_dram", array.shape, _mybir.dt.from_np(array.dtype), kind="ExternalInput").ap()
    out = nc.dram_tensor("out_0_dram", (1, LAT, D), F32, kind="ExternalOutput").ap()
    build(nc, aps, aps["rope_cos"], aps["rope_sin"], out)
    r = _run(nc, [arrays], core_ids=[0])
    return r.results[0]["out_0_dram"]
```

```python
from contextlib import ExitStack

import concourse.bass as bass
from concourse import mybir

ALU = mybir.AluOpType
ACT = mybir.ActivationFunctionType
AX_X = mybir.AxisListType.X
F32 = mybir.dt.float32
U32 = mybir.dt.uint32

P = 128
D = 1024
KD = D // P
DEPTH = 2
LAT, CTXL = 512, 256
NLAT, NCTX = LAT // P, CTXL // P
NB = NLAT + NCTX
TOK = LAT + CTXL
EPS = 1e-6
HD = 64
NQ, NKV = 8, 2
REP = NQ // NKV
AW, KW = NQ * HD, NKV * HD
QKV = AW + 2 * KW
GW = D // 4
CW = D // 4
GROUPS = 4
GC = GW // GROUPS
TAPS = 31
PAD = TAPS // 2
IN_W = QKV + 2 * GW + 2 * CW
U_AT, V_AT = QKV, QKV + GW
A_AT, G_AT = QKV + 2 * GW, QKV + 2 * GW + CW
PH = 8
NK = 128
TOPK = 16
NEXP = NK * NK
SLOTS = PH * TOPK
ALPHA = float((2 * DEPTH) ** 0.25)
SCALE = float(HD ** -0.5)
LOWEST = -3.0e38
MODC = 6 * D // 512
INC, INW = 4, IN_W // 4
OUTC = D // 512
QC = 2 * PH * P // 512
WCHUNKS = MODC + INC + OUTC + QC
BW = 256
FIRSTC = 2 * D // 512
BQC = 2 * PH * P // BW
BMC = 6 * D // BW
HALF = TOPK // 2
UR = 8
BLOCKS = [NB, NLAT]
EARLY = [(LAT, TOK), (0, P)]
LATER = [(0, LAT), (P, LAT)]


class Chain:

    def __init__(self, eng, sem, base=0):
        self.eng, self.sem, self.base, self.n, self.counts = eng, sem, base, 0, {}

    def __call__(self, ins):
        ins.then_inc(self.sem, 1)
        self.n += 1
        self.eng.wait_ge(self.sem, self.base + self.n)

    def post(self, ins):
        ins.then_inc(self.sem, 1)
        self.n += 1
        return self.base + self.n

    def need(self, count):
        self.eng.wait_ge(self.sem, count)

    def sig(self, ins, sem):
        ins.then_inc(sem, 1)
        self.counts[sem.name] = self.counts.get(sem.name, 0) + 1
        self.eng.wait_ge(sem, self.counts[sem.name])


PER_BLOCK = {"g_idx": PH, "g_ud": SLOTS, "g_gel": PH, "g_w": PH, "g_dg": SLOTS, "g_vd": SLOTS, "g_y": 2, "g_best": PH,
             "g_h": 1, "lo_sig": 1, "lo_gelu": 1, "lo_glu": 1, "lo_gt": 1, "lo_cin": 1, "lo_vn": 1, "lo_gm": 1, "lo_yg": 1, "lo_ygt": 1,
             "lo_yge": 1, "lo_ct": 1, "lo_cy": 1, "lo_cn": 1, "lo_silu": 1, "lo_st": 1, "lo_se": 1, "ph_h": 1, "ph_tr": 1, "ph_hev": 2,
             "ou_mm": OUTC, "ou_ev": OUTC}


def top_steps(block0):
    if block0:
        return {1: [(0, 2), (0, 3)], 2: [(0, 4), (0, 5)], 3: [(0, 6), (0, 7)], 4: [(1, 0), (1, 1)], 5: [(1, 2), (1, 3)],
                6: [(1, 4)], 7: [(1, 5)], 8: [(1, 6)]}
    return {h: [(0, PH - 1)] if h == 1 else [(1, h - 2)] for h in range(1, PH + 1)}


PER_LAYER = {"bmod": 16, "mod_mm": MODC, "mod_ev": MODC, "mod_st": 16, "mbc_in": 64, "gqk": 32, "row_ld": 64, "lo_ld": 96, "mbc_out": 32,
             "mbc_sc2": 32, "mbc_sh2": 32, "mbc_g2": 32, "lnbc": 32, "lnbc2": 32, "sk_ld": 16, "in_h": NB, "in_tr": NB, "in_hev": 2 * NB,
             "at_q": NB, "at_tr": NB, "at_qev": NB, "q_mm": 2 * PH, "q_ev": 2 * PH, "q_s": 2 * PH,
             "b_mm": 2 * PH, "b_ev": 2 * PH, "b_s": 2 * PH, "m_mm": 0, "m_ev": 0, "sk_tr": 4, "sk_ev": 4}


class Signals:

    def __init__(self, layer, sems):
        self.layer, self.sems = layer, sems

    def __getitem__(self, name):
        return self.sems[name]

    def at(self, name, count):
        before = PER_BLOCK.get(name, 0) * sum(BLOCKS[:self.layer]) + PER_LAYER.get(name, 0) * self.layer
        return self.sems[name], before + count


def chunk_number(layer, kind, i):
    first = {"mod": 0, "in": MODC, "out": MODC + INC, "q": MODC + INC + OUTC}[kind]
    return layer * WCHUNKS - MODC * layer + first + i


def place_of(layer, t):
    return (t + NCTX) % NB if BLOCKS[layer] == NB else t


def block_at(layer, place):
    return (place + NLAT) % NB if BLOCKS[layer] == NB else place


def blocks_of(tokens):
    return range(tokens[0] // P, tokens[1] // P)


def in_tiles(layer):
    return [(c, t) for c in range(INC) for t in range(NB) if t < BLOCKS[layer] or (c * INW < AW + 2 * KW and (c + 1) * INW > AW)]


def in_owner(tile):
    c, t = tile
    return "dve" if c == 1 and t % 2 else "act"


def att_units(layer):
    units = [(0, NLAT, h, t) for h in range(NQ) for t in range(NLAT)]
    if BLOCKS[layer] == NB:
        units += [(NLAT, NCTX, h, t) for h in range(NQ) for t in range(NLAT, NB)]
    return units


def build(nc, a, rope_cos, rope_sin, out):
    with ExitStack() as ctx:
        def sb(name, shape, dt=F32):
            return ctx.enter_context(nc.sbuf_tensor(name, shape, dt))

        def sem(name):
            return ctx.enter_context(nc.semaphore(name))

        X = sb("X", [P, NB, D])
        hT = sb("hT", [P, KD, TOK])
        W = sb("W", [P, 2, KD * 512])
        modbc = sb("modbc", [P, 2, 2, D])
        lnbc = sb("lnbc", [P, 2, D])
        ident = sb("ident", [P, P])
        iota16 = sb("iota16", [P, TOPK])
        cosT = sb("cosT", [P, NLAT, 2, 16])
        sinT = sb("sinT", [P, NLAT, 2, 16])
        cond = sb("cond", [P, 2, KD])
        eps = sb("eps", [P, 1])
        st = sb("st", [P, NB, 2, 6])
        mv = sb("mv", [P, NB, 2])
        sd = sb("sd", [P, NB * 10])
        rstd = sb("rstd", [P, NB * 10])
        tiny = sb("tiny", [P, 16])
        gsum = sb("gsum", [P, PH])
        scr = sb("scr", [P, P])
        cols = sb("cols", [P, GROUPS + 2 * (TAPS + 2)])
        ARENA = 25472
        arena = sb("arena", [P, ARENA])
        PS = ctx.enter_context(nc.psum_tensor("PS", [P, 8, 512], F32))
        PSf = PS[:, :, :].rearrange("p b n -> p (b n)")
        modd = nc.dram_tensor("modd", (DEPTH, 2, 6 * D), F32).ap()

        def carve(*spec):
            at, views = 0, []
            for dims in spec:
                n = 1
                for x in dims:
                    n *= x
                v = arena[:, at:at + n]
                at += n
                if len(dims) == 2:
                    v = v.rearrange("p (a b) -> p a b", a=dims[0])
                if len(dims) == 3:
                    v = v.rearrange("p (a b c) -> p a b c", a=dims[0], b=dims[1])
                views.append(v)
            assert at <= ARENA, at
            return views

        wv = [W[:, s, :].rearrange("p (k n) -> p k n", k=KD) for s in range(2)]
        modrow, = carve([6 * D])
        bmod = hT[:, :, :].rearrange("p k n -> p (k n)")
        MIX = [NB, IN_W], [REP, TOK], [TOK]
        proj, hb = carve([NB, IN_W], [2, D])
        _, qT, kT, probs, probsT, cin, cacc = carve(*MIX, [2, TOK], [2, NB * LAT], [2, TOK + 4 * PAD], [2, TOK])
        _, _, _, qn, tA, tB, qr, gqk, rows, bsr = carve(*MIX, [10, HD], [320], [320], [NB, 10 * HD], [10, HD], [CW], [P])
        _, cy, sT, ws, wsT, wpw, gln, cln = carve([NB, IN_W], [NB, CW], [2, TOK], [GROUPS, P], [GROUPS, P], [2, CW], [2, GW], [2, CW])
        H2, V16, I16f, sk, qs, shift2, spare = carve([NB, D], [NB, 2 * PH * TOPK], [NB, 2 * PH * TOPK], [2 * PH, P], [2, TOK], [2, D], [2, 512])
        _, _, _, vring, hcur, cand, eq, dg, best, gate, actv, gel, wgt, idxf, pos, hilo, e12, skT, qs2, gate2 = carve(
            [NB, D], [NB, 2 * PH * TOPK], [NB, 2 * PH * TOPK], [UR, D], [D], [TOPK * TOPK], [TOPK * TOPK], [4, P],
            [SLOTS], [SLOTS], [SLOTS], [SLOTS], [SLOTS], [SLOTS], [TOPK], [2 * TOPK], [2 * TOPK],
            [2 * PH, P], [2, LAT], [2, D])
        brow = qs2
        bring = modbc[:, :, :, :].rearrange("p s r (q n) -> p s (r q) n", n=BW)
        modrow2 = hT[:, :, :].rearrange("p k n -> p (k n)")
        I16 = I16f.bitcast(U32)
        idx = idxf.bitcast(U32)
        pos = pos.bitcast(U32)
        hilo = hilo.bitcast(U32)
        uring = W[:, :, :].rearrange("p s (r d) -> p (s r) d", d=D)
        H2f = H2.rearrange("p b d -> p (b d)")
        V16f = V16.rearrange("p b n -> p (b n)")
        I16f = I16.rearrange("p b n -> p (b n)")

        s_phase = sem("s_phase")
        s_const = sem("s_const")
        s_eps = sem("s_eps")
        s_load0 = sem("s_load0")
        s_rest = sem("s_rest")
        s_cload = sem("s_cload")
        s_cond = sem("s_cond")
        s_wfull = [sem(f"s_wfull{i}") for i in range(2)]
        c_dve = sem("c_dve")
        c_pool = sem("c_pool")
        s_bfull = [sem(f"s_bfull{i}") for i in range(2)]
        s_out = sem("s_out")
        names = ["bmod", "mod_mm", "mod_ev", "mod_st", "mbc_in", "stat", "root", "in_h", "in_tr", "in_hev", "in_mm", "in_eva", "in_evd",
                 "gqk", "row_ld", "mbc_out", "mbc_sc2", "lnbc", "at_q", "at_tr", "at_qev", "at_s", "at_max", "at_exp", "at_rcp", "at_nrm", "at_t", "at_tev",
                 "at_pv", "at_oev", "lo_ld", "lo_rt", "lo_rev", "lo_wt", "lo_wev", "lo_sig", "lo_gelu", "lo_glu", "lo_gt", "lo_cin", "lo_vn", "lo_gm",
                 "lo_yg", "lo_ygt", "lo_yge", "lo_tap", "lo_ct", "lo_cy", "lo_cn", "lo_silu", "lo_st", "lo_se", "lo_pw", "lo_pwe",
                 "ou_mm", "ou_ev", "mbc_sh2", "ph_h", "ph_tr", "ph_hev", "sk_ld", "sk_tr", "sk_ev", "q_mm", "q_ev", "q_s", "q_tk", "b_mm", "b_ev", "b_s", "b_tk", "m_mm", "m_ev",
                 "g_idx", "g_ud", "g_gel", "g_w", "g_dg", "g_vd", "g_y", "g_best", "mbc_g2", "lnbc2", "ep", "g_h"]
        shared = {n: sem(n) for n in (*PER_BLOCK, *PER_LAYER)}
        S = [Signals(layer, {n: shared[n] if n in shared else sem(f"{n}_{layer}") for n in names}) for layer in range(DEPTH)]
        s_u = [sem(f"s_u{r}") for r in range(UR)]
        s_v = [sem(f"s_v{r}") for r in range(UR)]
        c_tk = sem("c_tk")
        s_hold = sem("s_hold")
        c_up = sem("c_up")
        passed = [sem(f"passed{i}") for i in range(2)]

        ENGINES = 4

        def phase_end(eng, n):
            eng.drain().then_inc(s_phase, 1)
            eng.wait_ge(s_phase, ENGINES * n)

        block = ctx.enter_context(nc.Block())

        @block.sync
        def _(sp):
            def load(n, kind, src, width, free):
                slot = n % 2
                rows = src.rearrange("(p k) n -> p k n" if kind == "mod" else "(k p) n -> p k n", p=P)
                if free is not None:
                    sp.wait_ge(*free)
                sp.dma_start(wv[slot][:, :, 0:width], rows).then_inc(s_wfull[slot], 16)

            def done(layer, kind, i):
                q = S[layer]
                if kind == "mod":
                    return q.at("mod_mm", i + 1)
                if kind == "in":
                    return q.at("in_mm", max(n for n, (c, t) in enumerate(in_tiles(layer)) if c == i) + 1)
                if kind == "out":
                    return q.at("ou_mm", OUTC * (BLOCKS[layer] - 1) + i + 1)
                return q.at("q_mm", 4 * (i + 1))

            beside = [0]
            used = []

            def load_beside(parts, free):
                m = beside[0]
                if m >= 2:
                    sp.wait_ge(*used[m - 2])
                for dst, src in parts(m % 2):
                    sp.dma_start(dst, src).then_inc(s_bfull[m % 2], 16)
                used.append(free)
                beside[0] += 1

            for layer in range(DEPTH):
                q = S[layer]
                order = [(layer, "mod", i, a["w_mod"][layer][:, i * 512:(i + 1) * 512], 512) for i in range(MODC if layer == 0 else 0)]
                order += [(layer, "in", i, a["w_in"][layer][:, i * INW:(i + 1) * INW], INW) for i in range(INC)]
                order += [(layer, "out", i, a["w_out"][layer][:, i * 512:(i + 1) * 512], 512) for i in range(OUTC)]
                order += [(layer, "q", i, a["peer_w_q"][layer][:, i * 512:(i + 1) * 512], 512) for i in range(QC)]
                for n, (_, kind, i, src, width) in enumerate(order):
                    if n >= 2:
                        free = done(*order[n - 2][:3])
                    else:
                        free = S[layer - 1].at("g_ud", SLOTS * BLOCKS[layer - 1]) if layer else None
                    load(chunk_number(layer, kind, i), kind, src, width, free)
                    if kind == "mod" and i == FIRSTC + 1:
                        sp.wait_ge(*q.at("mod_ev", FIRSTC))
                        sp.dma_start(modd[layer, :, 0:2 * D], modrow[0:2, 0:2 * D]).then_inc(q["mod_st"], 16)
                    if kind == "mod" and i == MODC - 1:
                        sp.wait_ge(*q.at("mod_ev", MODC))
                        sp.dma_start(modd[layer, :, 2 * D:6 * D], modrow[0:2, 2 * D:6 * D]).then_inc(s_rest, 16)
                sp.wait_ge(*q.at("ph_h", BLOCKS[layer]))
                for i in range(BQC):
                    load_beside(lambda slot: [(bring[:, slot, :, :], a["peer_w_q"][layer][:, i * BW:(i + 1) * BW].rearrange("(k p) n -> p k n", p=P))],
                                q.at("b_mm", BW // P * (i + 1)))
                if layer + 1 < DEPTH:
                    sp.wait_ge(*q.at("b_s", 2 * PH))
                    for i in range(BMC):
                        if i >= 2:
                            sp.wait_ge(*q.at("m_ev", i - 1))
                        cs = slice(i * BW, (i + 1) * BW)
                        load_beside(lambda slot: [(bring[:, slot, :, :], a["w_mod"][layer + 1][:, cs].rearrange("(p k) n -> p k n", p=P)),
                                                  (brow[0:2, slot, 0:BW], a["b_mod"][layer + 1, cs].partition_broadcast(2))],
                                    q.at("m_mm", i + 1))
                    sp.wait_ge(*q.at("m_ev", BMC))
                    sp.dma_start(modd[layer + 1], modrow2[0:2, :]).then_inc(S[layer + 1]["mod_st"], 16)
            for t in range(NLAT):
                sp.wait_ge(*S[DEPTH - 1].at("ep", t + 1))
                sp.dma_start(out[0, t * P:(t + 1) * P, :], X[:, t, :]).then_inc(s_out, 16)
            sp.wait_ge(s_out, 16 * NLAT)

        @block.gpsimd
        def _(pool):
            ch = Chain(pool, c_pool)
            ch(pool.iota(ident[:, :], [[1, P]], base=0, channel_multiplier=-1, allow_small_or_imprecise_dtypes=True))
            pool.iota(iota16[:, :], [[1, TOPK]], base=0, channel_multiplier=0, allow_small_or_imprecise_dtypes=True).then_inc(s_const, 1)
            pool.tensor_scalar(ident[:, :], ident[:, :], 0.0, None, ALU.is_equal).then_inc(s_const, 1)
            pool.dma_start(cond[:, 0, :], a["c"][0].rearrange("(p k) -> p k", p=P)).then_inc(s_cload, 16)
            pool.dma_start(cond[:, 1, :], a["c_ctx"].rearrange("(p k) -> p k", p=P)).then_inc(s_cload, 16)
            pool.wait_ge(s_wfull[0], 16)
            pool.dma_start(X[:, 0:NLAT, :], a["x"][0].rearrange("(b p) d -> p b d", p=P)).then_inc(s_load0, 16)
            pool.dma_start(X[:, NLAT:NB, :], a["ctx"][0].rearrange("(b p) d -> p b d", p=P)).then_inc(s_load0, 16)
            pool.dma_start(cosT[:, :, :, :].rearrange("p b a f -> p b (a f)"), rope_cos.rearrange("(b p) f -> p b f", p=P)).then_inc(s_load0, 16)
            pool.dma_start(sinT[:, :, :, :].rearrange("p b a f -> p b (a f)"), rope_sin.rearrange("(b p) f -> p b f", p=P)).then_inc(s_load0, 16)
            pool.wait_ge(s_load0, 64)

            def rows_to(dst, src, done):
                pool.dma_start(dst, src.partition_broadcast(P)).then_inc(done, 16)

            def modulation_row(layer, stream, part, slot, done):
                rows_to(modbc[:, stream, slot, :], modd[layer, stream, part * D:(part + 1) * D], done)

            def first_rows(layer):
                pool.wait_ge(*S[layer].at("mod_st", 16))
                for stream in range(2):
                    for part in range(2):
                        modulation_row(layer, stream, part, part, S[layer]["mbc_in"])

            n = 0
            for layer in range(DEPTH):
                q = S[layer]
                if layer == 0:
                    pool.dma_start(bmod[0:2, :], a["b_mod"][layer].partition_broadcast(2)).then_inc(q["bmod"], 16)
                    first_rows(layer)
                    pool.wait_ge(s_rest, 16)
                    n += 1
                    phase_end(pool, n)
                for dst, src in ((rows[0:TAPS, :], a["conv_w_dw"][layer]),
                                 (rows[TAPS:TAPS + 1, :], a["conv_b_dw"][layer:layer + 1, :]),
                                 (rows[TAPS + 1:TAPS + 2, :], a["conv_b_pw"][layer:layer + 1, :]),
                                 (bsr[0:GROUPS, :], a["gmlp_b_s"][layer])):
                    pool.dma_start(dst, src).then_inc(q["row_ld"], 16)
                pool.dma_start(gqk[:, 0:NQ, :], a["q_norm_g"][layer].partition_broadcast(P).unsqueeze(1).to_broadcast([P, NQ, HD])).then_inc(q["gqk"], 16)
                pool.dma_start(gqk[:, NQ:NQ + NKV, :], a["k_norm_g"][layer].partition_broadcast(P).unsqueeze(1).to_broadcast([P, NKV, HD])).then_inc(q["gqk"], 16)
                n += 1
                phase_end(pool, n)
                for stream in range(2):
                    modulation_row(layer, stream, 2, 0, q["mbc_out"])
                    modulation_row(layer, stream, 4, 1, q["mbc_sc2"])
                rows_to(lnbc[:, 0, :], a["ln1_g"][layer], q["lnbc"])
                rows_to(lnbc[:, 1, :], a["ln1_b"][layer], q["lnbc"])
                n += 1
                phase_end(pool, n)
                for dst, src in ((ws, a["gmlp_w_s"][layer].rearrange("g p q -> p g q")),
                                 (wpw, a["conv_w_pw"][layer].rearrange("(k p) n -> p k n", p=P))):
                    pool.dma_start(dst, src).then_inc(q["lo_ld"], 16)
                for dst, src in ((gln[:, 0, :], a["gmlp_ln_g"][layer]), (gln[:, 1, :], a["gmlp_ln_b"][layer]),
                                 (cln[:, 0, :], a["conv_ln_g"][layer]), (cln[:, 1, :], a["conv_ln_b"][layer])):
                    rows_to(dst, src, q["lo_ld"])
                n += 1
                phase_end(pool, n)
                pool.dma_start(sk, a["peer_sub_keys"][layer].rearrange("h s k d -> k (h s) d")).then_inc(q["sk_ld"], 16)
                for stream in range(2):
                    rows_to(shift2[:, stream, :], modd[layer, stream, 3 * D:4 * D], q["mbc_sh2"])
                n += 1
                phase_end(pool, n)
                for stream in range(2):
                    rows_to(gate2[:, stream, :], modd[layer, stream, 5 * D:6 * D], q["mbc_g2"])
                rows_to(lnbc[:, 0, :], a["ln2_g"][layer], q["lnbc2"])
                rows_to(lnbc[:, 1, :], a["ln2_b"][layer], q["lnbc2"])
                n += 1
                phase_end(pool, n)
                pu, pv = a["peer_u"], a["peer_v"]
                nblk = BLOCKS[layer]
                base = sum(BLOCKS[:layer])

                def gather(ring, slot, table, column, done):
                    pool.indirect_dma_start(ring[:, slot, :], None, table,
                                            bass.IndirectOffsetOnAxis(ap=idx[:, column:column + 1], axis=0)).then_inc(done[slot], 16)

                def hold(s, value):
                    pool.wait_ge(s, value)
                    if not isinstance(value, int):
                        pool.sem_inc(passed[0], 1)

                def u_rows(b, h, first=False):
                    hold(*q.at("g_idx", b * PH + h + 1))
                    for k in range(TOPK):
                        if not (first and k < UR):
                            hold(*q.at("g_ud", b * SLOTS + h * TOPK + k - UR + 1))
                        gather(uring, k % UR, pu, (h % PH) * TOPK + k, s_u)
                        yield

                def v_rows(b, h, first=False):
                    for k in range(TOPK):
                        if not (first and k < UR):
                            hold(*q.at("g_vd", b * SLOTS + h * TOPK + k - UR + 1))
                        gather(vring, k % UR, pv, h * TOPK + k, s_v)
                        yield

                def both(*streams):
                    streams = list(streams)
                    while streams:
                        for s in list(streams):
                            if next(s, "end") == "end":
                                streams.remove(s)

                def body(b, last, first=False):
                    for h in range(1, PH):
                        both(u_rows(b, h), v_rows(b, h - 1, first and h == 1))
                    if last:
                        both(v_rows(b, PH - 1))
                    else:
                        both(u_rows(b, PH), v_rows(b, PH - 1))

                both(u_rows(0, 0, True))
                body(0, False, True)
                body(1, False)
                with pool.Fori(2, nblk - 1) as b:
                    body(b, False)
                body(nblk - 1, True)
                if layer + 1 < DEPTH:
                    first_rows(layer + 1)
                n += 1
                phase_end(pool, n)

        @block.scalar
        def _(act):
            def copy(dst, src):
                return act.activation(dst, src, ACT.Copy)

            act.wait_ge(s_cload, 32)
            act.activation(cond[:, :, :], cond[:, :, :], ACT.Silu).then_inc(s_cond, 1)
            act.wait_ge(s_eps, 1)
            roots = [0]
            n = 0

            def root(layer, count, scale=1.0, src=None, at=0):
                roots[0] += 1
                act.wait_ge(*S[layer].at("stat", roots[0]))
                act.activation(sd[:, at:at + count], mv[:, 0:count, 1] if src is None else src, ACT.Sqrt, bias=eps[:, 0:1],
                               scale=scale).then_inc(S[layer]["root"], 1)

            for layer in range(DEPTH):
                q = S[layer]
                nblk = BLOCKS[layer]
                roots[0] = 0
                root(layer, NB)
                if layer == 0:
                    n += 1
                    phase_end(act, n)
                tiles = in_tiles(layer)

                def in_evac(i):
                    c, t = tiles[i]
                    act.wait_ge(*q.at("in_mm", i + 1))
                    copy(proj[:, t, c * INW:(c + 1) * INW], PS[:, 4 + i % 4, 0:INW]).then_inc(q["in_eva"], 1)

                chunk0 = [i for i, (c, t) in enumerate(tiles) if c == 0]
                chunk2 = [i for i, (c, t) in enumerate(tiles) if c == 2]
                for t in range(NB):
                    act.wait_ge(*q.at("in_tr", t + 1))
                    for j in range(2):
                        copy(hT[:, 4 * j:4 * j + 4, t * P:(t + 1) * P],
                             PS[:, 2 * (t % 2) + j, :].rearrange("p (k n) -> p k n", k=4)).then_inc(q["in_hev"], 1)
                    if t < len(chunk0):
                        in_evac(t)
                for i in range(len(chunk0), len(tiles)):
                    if in_owner(tiles[i]) == "act":
                        in_evac(i)
                    if i == chunk2[2]:
                        root(layer, NB * 10, 1.0 / HD, rstd[:, :])
                act.wait_ge(*q.at("lo_rt", 1))
                copy(cols[:, :], PS[:, 0, 0:GROUPS + 2 * (TAPS + 2)]).then_inc(q["lo_rev"], 1)
                act.wait_ge(q["in_eva"], sum(in_owner(x) == "act" for x in tiles))
                for t in range(nblk):
                    act.activation(proj[:, t, G_AT:G_AT + CW], proj[:, t, G_AT:G_AT + CW], ACT.Sigmoid).then_inc(q["lo_sig"], 1)
                for t in range(NB):
                    act.wait_ge(*q.at("at_tr", t + 1))
                    if t < nblk:
                        copy(qT[:, :, t * P:(t + 1) * P], PS[:, 2 * (t % 2), :].rearrange("p (j n) -> p j n", j=REP))
                    copy(kT[:, t * P:(t + 1) * P], PS[:, 2 * (t % 2) + 1, 0:P]).then_inc(q["at_qev"], 1)

                def place(t):
                    return PAD + t * P if t < NLAT else 3 * PAD + t * P

                for t in range(nblk):
                    act.wait_ge(*q.at("lo_gt", t + 1))
                    copy(cin[:, :, place(t):place(t) + P], PS[:, 4 + t % 2, 0:CW].rearrange("p (c n) -> p c n", c=2)).then_inc(q["lo_cin"], 1)
                n += 1
                phase_end(act, n)
                units = att_units(layer)

                def keys_of(first):
                    return range(NB) if first == 0 else range(NLAT, NB)

                def evac_probs(i):
                    first, m, h, t = units[i]
                    kb = len(keys_of(first))
                    if t == first and head_no(i) >= 2:
                        act.wait_ge(*q.at("at_pv", head_no(i) - 1))
                    act.wait_ge(*q.at("at_t", i + 1))
                    copy(probsT[:, head_no(i) % 2, :].rearrange("p (k n) -> p k n", k=NB)[:, 0:kb, (t - first) * P:(t - first + 1) * P],
                         PSf[:, 4 * 512:4 * 512 + kb * P].rearrange("p (k n) -> p k n", k=kb)).then_inc(q["at_tev"], 1)

                def head_no(i):
                    first, m, h, t = units[i]
                    return h if first == 0 else NQ + h

                def evac_out(i):
                    first, m, h, t = units[i]
                    pair = head_no(i) // 2
                    act.wait_ge(*q.at("at_pv", head_no(i) + 1))
                    copy(hT[:, h // 2, first * P:(first + m) * P], PS[:, 6 + pair % 2, 0:m * P]).then_inc(q["at_oev"], 1)

                def pair_end(i):
                    first, m, h, t = units[i]
                    return t == first + m - 1 and h % 2 == 1

                for i in range(len(units)):
                    first, m, h, t = units[i]
                    nk = len(keys_of(first)) * P
                    act.wait_ge(*q.at("at_max", i + 1))
                    if i >= 2:
                        act.wait_ge(*q.at("at_t", i - 1))
                    act.activation(probs[:, i % 2, 0:nk], PSf[:, (i % 2) * 1024:(i % 2) * 1024 + nk], ACT.Exp, bias=tiny[:, i % 4:i % 4 + 1],
                                   scale=SCALE, accum_out=tiny[:, 4 + i % 4:5 + i % 4]).then_inc(q["at_exp"], 1)
                    if i >= 1:
                        evac_probs(i - 1)
                    act.wait_ge(*q.at("at_rcp", i + 1))
                    act.activation(probs[:, i % 2, 0:nk], probs[:, i % 2, 0:nk], ACT.Copy, scale=tiny[:, 8 + i % 4:9 + i % 4]).then_inc(q["at_nrm"], 1)
                    if i >= 3 and pair_end(i - 3):
                        evac_out(i - 3)
                evac_probs(len(units) - 1)
                for i in range(len(units) - 3, len(units)):
                    if pair_end(i):
                        evac_out(i)
                n += 1
                phase_end(act, n)
                act.wait_ge(*q.at("lo_wt", 1))
                copy(wsT, PS[:, 0, :].rearrange("p (g n) -> p g n", g=GROUPS)).then_inc(q["lo_wev"], 1)
                for t in range(nblk):
                    act.activation(proj[:, t, U_AT:U_AT + 2 * GW], proj[:, t, U_AT:U_AT + 2 * GW], ACT.Gelu_apprx_tanh).then_inc(q["lo_gelu"], 1)
                root(layer, nblk)
                for t in range(nblk):
                    act.wait_ge(*q.at("lo_ct", t + 1))
                    copy(cy[:, t, :], PS[:, 2 + t % 2, 0:CW]).then_inc(q["lo_cy"], 1)
                root(layer, nblk)
                for t in range(nblk):
                    act.wait_ge(*q.at("lo_ygt", t + 1))
                    copy(hT[:, 4:6, t * P:(t + 1) * P], PS[:, t % 2, 0:CW].rearrange("p (k n) -> p k n", k=2)).then_inc(q["lo_yge"], 1)
                for t in range(nblk):
                    act.wait_ge(*q.at("lo_cn", t + 1))
                    act.activation(cy[:, t, :], cy[:, t, :], ACT.Silu).then_inc(q["lo_silu"], 1)
                for t in range(nblk):
                    act.wait_ge(*q.at("lo_st", t + 1))
                    copy(sT[:, :, t * P:(t + 1) * P], PS[:, t % 2, 0:CW].rearrange("p (k n) -> p k n", k=2)).then_inc(q["lo_se"], 1)
                for mo in range(2):
                    bias = cols[:, GROUPS + mo * (TAPS + 2) + TAPS + 1:GROUPS + mo * (TAPS + 2) + TAPS + 2]
                    for s, (t0, t1) in enumerate(((0, LAT), (LAT, TOK))[:1 + (nblk == NB)]):
                        act.wait_ge(*q.at("lo_pw", mo * (1 + (nblk == NB)) + s + 1))
                        act.activation(hT[:, 6 + mo, t0:t1], PS[:, 2 + 2 * mo + s, 0:t1 - t0], ACT.Identity, bias=bias).then_inc(q["lo_pwe"], 1)
                n += 1
                phase_end(act, n)
                for j in range(4):
                    act.wait_ge(*q.at("sk_tr", j + 1))
                    copy(skT[:, 4 * j:4 * j + 4, :], PS[:, 4 + j, :].rearrange("p (k n) -> p k n", k=4)).then_inc(q["sk_ev"], 1)

                def peer_input(t):
                    act.wait_ge(*q.at("ph_tr", t + 1))
                    for j in range(2):
                        copy(hT[:, 4 * j:4 * j + 4, t * P:(t + 1) * P],
                             PS[:, 4 + 2 * (t % 2) + j, :].rearrange("p (k n) -> p k n", k=4)).then_inc(q["ph_hev"], 1)

                for t in range(nblk):
                    root(layer, 1, 1.0, mv[:, t, 1:2])
                    root(layer, 1, 1.0, mv[:, t, 1:2])
                    if t >= 2:
                        peer_input(t - 2)
                peer_input(nblk - 2)
                peer_input(nblk - 1)
                n += 1
                phase_end(act, n)
                early = EARLY[layer][1] - EARLY[layer][0]
                later = LATER[layer][1] - LATER[layer][0]
                for hp in range(2 * PH):
                    act.wait_ge(*q.at("q_mm", hp + 1))
                    if hp >= 2:
                        act.wait_ge(*q.at("q_s", hp - 1))
                    copy(qs[:, hp % 2, 0:early], PS[:, hp % 2, 0:early]).then_inc(q["q_ev"], 1)
                n += 1
                phase_end(act, n)

                def gates(b, h):
                    act.wait_ge(*q.at("g_best", b * PH + h + 1))
                    act.activation(gate[:, h * TOPK:(h + 1) * TOPK], gate[:, h * TOPK:(h + 1) * TOPK], ACT.Exp,
                                   accum_out=gsum[:, h:h + 1])

                def gelu(b, h):
                    act.wait_ge(*q.at("g_ud", b * SLOTS + (h + 1) * TOPK))
                    act.activation(gel[:, h * TOPK:(h + 1) * TOPK], actv[:, h * TOPK:(h + 1) * TOPK], ACT.Gelu_apprx_tanh).then_inc(q["g_gel"], 1)

                def diagonals(b, h, lo, hi, first=False):
                    if lo == 0:
                        act.wait_ge(*q.at("g_w", b * PH + h + 1))
                    for k in range(lo, hi):
                        if not (first and k < 4):
                            act.wait_ge(*q.at("g_vd", b * SLOTS + h * TOPK + k - 3))
                        act.activation(dg[:, k % 4, :], ident[:, :], ACT.Copy, scale=wgt[:, h * TOPK + k:h * TOPK + k + 1]).then_inc(q["g_dg"], 1)

                def beside():
                    for hp in range(2 * PH):
                        act.wait_ge(*q.at("b_mm", hp + 1))
                        if hp >= 2:
                            act.wait_ge(*q.at("b_s", hp - 1))
                        copy(qs2[:, hp % 2, 0:later], PS[:, 2 + hp % 2, 0:later]).then_inc(q["b_ev"], 1)
                        yield

                waiting = beside()

                def y_out(b):
                    act.wait_ge(*q.at("g_vd", (b + 1) * SLOTS))
                    if not isinstance(b, int):
                        act.sem_inc(passed[1], 1)
                    for j in range(2):
                        dst = H2f[:, bass.ds(b * D + j * 512, 512)] if not isinstance(b, int) else H2f[:, b * D + j * 512:b * D + j * 512 + 512]
                        copy(dst, PS[:, j, :]).then_inc(q["g_y"], 1)

                def close():
                    yield
                    for p in range(nblk - 1):
                        root(layer, 1, 1.0, mv[:, p, 1:2], p)
                        yield

                def body(b, last, first=False):
                    extra = close() if last else waiting
                    for h in range(1, PH + 1):
                        gelu(b, h - 1)
                        diagonals(b, h - 1, 0, HALF, first and h == 1)
                        next(extra, None)
                        diagonals(b, h - 1, HALF, TOPK)
                        next(extra, None)
                        for ahead, hh in top_steps(first)[h]:
                            if ahead == 0 or not last:
                                gates(b + ahead, hh)
                    y_out(b)

                gates(0, 0)
                gates(0, 1)
                body(0, False, True)
                body(1, False)
                with act.Fori(2, nblk - 1) as b:
                    body(b, False)
                body(nblk - 1, True)
                root(layer, 1, 1.0, mv[:, nblk - 1, 1:2], nblk - 1)
                n += 1
                phase_end(act, n)

        @block.tensor
        def _(pe):
            def weights(layer, kind, i):
                n = chunk_number(layer, kind, i)
                pe.wait_ge(s_wfull[n % 2], 16 * (n // 2 + 1))
                return wv[n % 2]

            pe.wait_ge(s_const, 2)
            pe.wait_ge(s_cond, 1)
            n = 0
            for layer in range(DEPTH):
                q = S[layer]
                nblk = BLOCKS[layer]
                for i in range(MODC if layer == 0 else 0):
                    w = weights(layer, "mod", i)
                    if i >= 2:
                        pe.wait_ge(*q.at("mod_ev", i - 1))
                    for k in range(KD):
                        mm = pe.matmul(PS[0:2, i % 2, :], cond[:, :, k], w[:, k, :], start=(k == 0), stop=(k == KD - 1))
                    mm.then_inc(q["mod_mm"], 1)
                if layer == 0:
                    n += 1
                    phase_end(pe, n)
                tiles = in_tiles(layer)

                def in_mm(i):
                    c, t = tiles[i]
                    w = weights(layer, "in", c)
                    if i >= 4:
                        j = i - 4
                        owner = in_owner(tiles[j])
                        pe.wait_ge(q["in_eva" if owner == "act" else "in_evd"], sum(in_owner(x) == owner for x in tiles[:j + 1]))
                    for k in range(KD):
                        mm = pe.matmul(PS[:, 4 + i % 4, 0:INW], hT[:, k, t * P:(t + 1) * P], w[:, k, 0:INW], start=(k == 0), stop=(k == KD - 1))
                    mm.then_inc(q["in_mm"], 1)

                chunk0 = [i for i, (c, t) in enumerate(tiles) if c == 0]
                for t in range(NB):
                    pe.wait_ge(*q.at("in_h", t + 1))
                    if t >= 2:
                        pe.wait_ge(*q.at("in_hev", 2 * (t - 1)))
                    for k in range(KD):
                        tr = pe.transpose(PS[:, 2 * (t % 2) + k // 4, (k % 4) * P:(k % 4 + 1) * P], hb[:, t % 2, k * P:(k + 1) * P], ident[:, :])
                    tr.then_inc(q["in_tr"], 1)
                    pe.wait_ge(*q.at("in_hev", 2 * (t + 1)))
                    if t < len(chunk0):
                        in_mm(t)
                for i in range(len(chunk0), len(tiles)):
                    in_mm(i)
                pe.wait_ge(*q.at("row_ld", 64))
                pe.transpose(PS[:, 0, 0:GROUPS], bsr[0:GROUPS, :], ident[0:GROUPS, 0:GROUPS])
                for c in range(2):
                    tr = pe.transpose(PS[:, 0, GROUPS + c * (TAPS + 2):GROUPS + (c + 1) * (TAPS + 2)], rows[0:TAPS + 2, c * P:(c + 1) * P],
                                      ident[0:TAPS + 2, 0:TAPS + 2])
                tr.then_inc(q["lo_rt"], 1)
                pe.wait_ge(*q.at("lo_rev", 1))
                for t in range(NB):
                    pe.wait_ge(*q.at("at_q", t + 1))
                    if t >= 2:
                        pe.wait_ge(*q.at("at_qev", t - 1))
                    src = qr[:, t, :]
                    if t < nblk:
                        for j in range(REP):
                            pe.transpose(PS[:, 2 * (t % 2), j * P:(j + 1) * P], src[:, j * P:(j + 1) * P], ident[:, :])
                    pe.transpose(PS[:, 2 * (t % 2) + 1, 0:P], src[:, AW:AW + KW], ident[:, :]).then_inc(q["at_tr"], 1)
                pe.wait_ge(q["in_eva"], sum(in_owner(x) == "act" for x in tiles))
                for t in range(nblk):
                    pe.wait_ge(*q.at("lo_glu", t + 1))
                    if t >= 2:
                        pe.wait_ge(*q.at("lo_cin", t - 1))
                    for c in range(2):
                        tr = pe.transpose(PS[:, 4 + t % 2, c * P:(c + 1) * P], proj[:, t, A_AT + c * P:A_AT + (c + 1) * P], ident[:, :])
                    tr.then_inc(q["lo_gt"], 1)
                n += 1
                phase_end(pe, n)
                units = att_units(layer)

                def keys_of(first):
                    return range(NB) if first == 0 else range(NLAT, NB)

                def scores(i):
                    first, m, h, t = units[i]
                    g, j = h // REP, h % REP
                    if i >= 2:
                        pe.wait_ge(*q.at("at_exp", i - 1))
                    k0, k1 = keys_of(first)[0] * P, (keys_of(first)[-1] + 1) * P
                    for part, at in enumerate(range(k0, k1, 512)):
                        end = min(at + 512, k1)
                        mm = pe.matmul(PS[:, 2 * (i % 2) + part, 0:end - at], qT[g * HD:(g + 1) * HD, j, t * P:(t + 1) * P],
                                       kT[g * HD:(g + 1) * HD, at:end], start=True, stop=True)
                    mm.then_inc(q["at_s"], 1)

                def turn(i):
                    first, m, h, t = units[i]
                    pe.wait_ge(*q.at("at_nrm", i + 1))
                    if i >= 1:
                        pe.wait_ge(*q.at("at_tev", i))
                    for k in range(len(keys_of(first))):
                        tr = pe.transpose(PSf[:, 4 * 512 + k * P:4 * 512 + (k + 1) * P], probs[:, i % 2, k * P:(k + 1) * P], ident[:, :])
                    tr.then_inc(q["at_t"], 1)

                def head_end(i):
                    first, m, h, t = units[i]
                    return t == first + m - 1

                def values(i):
                    first, m, h, t = units[i]
                    g = h // REP
                    no = h if first == 0 else NQ + h
                    pair = no // 2
                    pe.wait_ge(*q.at("at_tev", i + 1))
                    if pair >= 2 and no % 2 == 0:
                        pe.wait_ge(*q.at("at_oev", pair - 1))
                    kbs = list(keys_of(first))
                    for k, kb in enumerate(kbs):
                        mm = pe.matmul(PS[(h % 2) * HD:(h % 2 + 1) * HD, 6 + pair % 2, 0:m * P],
                                       proj[:, kb, AW + KW + g * HD:AW + KW + (g + 1) * HD],
                                       probsT[:, no % 2, :].rearrange("p (k n) -> p k n", k=NB)[:, k, 0:m * P],
                                       start=(k == 0), stop=(k == len(kbs) - 1), skip_group_check=True)
                    mm.then_inc(q["at_pv"], 1)

                scores(0)
                scores(1)
                for i in range(len(units)):
                    if i + 2 < len(units):
                        scores(i + 2)
                    turn(i)
                    if i >= 1 and head_end(i - 1):
                        values(i - 1)
                values(len(units) - 1)
                n += 1
                phase_end(pe, n)
                pe.wait_ge(*q.at("lo_ld", 96))
                for g in range(GROUPS):
                    tr = pe.transpose(PS[:, 0, g * P:(g + 1) * P], ws[:, g, :], ident[:, :])
                tr.then_inc(q["lo_wt"], 1)
                pe.wait_ge(*q.at("lo_wev", 1))
                for t in range(nblk):
                    pe.wait_ge(*q.at("lo_vn", t + 1))
                    for g in range(GROUPS):
                        mm = pe.matmul(PS[:, 4 + t // 2, (t % 2) * GW + g * GC:(t % 2) * GW + (g + 1) * GC], wsT[:, g, :],
                                       proj[:, t, V_AT + g * GC:V_AT + (g + 1) * GC], start=True, stop=True)
                    mm.then_inc(q["lo_gm"], 1)
                streams = 1 + (nblk == NB)
                pe.wait_ge(*q.at("lo_tap", TAPS * 2 * streams))
                for t in range(nblk):
                    if t >= 2:
                        pe.wait_ge(*q.at("lo_cy", t - 1))
                    for c in range(2):
                        tr = pe.transpose(PS[:, 2 + t % 2, c * P:(c + 1) * P], cacc[:, c, t * P:(t + 1) * P], ident[:, :])
                    tr.then_inc(q["lo_ct"], 1)
                for t in range(nblk):
                    pe.wait_ge(*q.at("lo_yg", t + 1))
                    if t >= 2:
                        pe.wait_ge(*q.at("lo_yge", t - 1))
                    for c in range(2):
                        tr = pe.transpose(PS[:, t % 2, c * P:(c + 1) * P], proj[:, t, U_AT + c * P:U_AT + (c + 1) * P], ident[:, :])
                    tr.then_inc(q["lo_ygt"], 1)
                pe.wait_ge(*q.at("lo_yge", nblk))
                for t in range(nblk):
                    pe.wait_ge(*q.at("lo_silu", t + 1))
                    if t >= 2:
                        pe.wait_ge(*q.at("lo_se", t - 1))
                    for c in range(2):
                        tr = pe.transpose(PS[:, t % 2, c * P:(c + 1) * P], cy[:, t, c * P:(c + 1) * P], ident[:, :])
                    tr.then_inc(q["lo_st"], 1)
                pe.wait_ge(*q.at("lo_se", nblk))
                for mo in range(2):
                    for s, (t0, t1) in enumerate(((0, LAT), (LAT, TOK))[:streams]):
                        for k in range(2):
                            mm = pe.matmul(PS[:, 2 + 2 * mo + s, 0:t1 - t0], wpw[:, k, mo * P:(mo + 1) * P], sT[:, k, t0:t1], start=(k == 0), stop=(k == 1))
                        mm.then_inc(q["lo_pw"], 1)
                n += 1
                phase_end(pe, n)
                wo = [weights(layer, "out", c) for c in range(OUTC)]

                def peer_input(t):
                    pe.wait_ge(*q.at("ph_h", t + 1))
                    if t >= 2:
                        pe.wait_ge(*q.at("ph_hev", 2 * (t - 1)))
                    for k in range(KD):
                        tr = pe.transpose(PS[:, 4 + 2 * (t % 2) + k // 4, (k % 4) * P:(k % 4 + 1) * P], H2[:, place_of(layer, t), k * P:(k + 1) * P], ident[:, :])
                    tr.then_inc(q["ph_tr"], 1)

                for t in range(nblk):
                    for c in range(OUTC):
                        i = t * OUTC + c
                        if i >= 4:
                            pe.wait_ge(*q.at("ou_ev", i - 3))
                        for k in range(KD):
                            mm = pe.matmul(PS[:, i % 4, :], hT[:, k, t * P:(t + 1) * P], wo[c][:, k, :], start=(k == 0), stop=(k == KD - 1))
                        mm.then_inc(q["ou_mm"], 1)
                    if t == 0:
                        pe.wait_ge(*q.at("sk_ld", 16))
                        for hp in range(2 * PH):
                            tr = pe.transpose(PS[:, 4 + hp // 4, (hp % 4) * P:(hp % 4 + 1) * P], sk[:, hp, :], ident[:, :])
                            if hp % 4 == 3:
                                tr.then_inc(q["sk_tr"], 1)
                    if t == 1:
                        pe.wait_ge(*q.at("sk_ev", 4))
                    if t >= 2:
                        peer_input(t - 2)
                peer_input(nblk - 2)
                peer_input(nblk - 1)
                n += 1
                phase_end(pe, n)
                e0, e1 = EARLY[layer]

                def queries(hp):
                    w = weights(layer, "q", hp // 4)
                    if hp >= 2:
                        pe.wait_ge(*q.at("q_ev", hp - 1))
                    for k in range(KD):
                        mm = pe.matmul(PS[:, hp % 2, 0:e1 - e0], w[:, k, (hp % 4) * P:(hp % 4 + 1) * P], hT[:, k, e0:e1],
                                       start=(k == 0), stop=(k == KD - 1))
                    mm.then_inc(q["q_mm"], 1)

                def key_scores(hp):
                    pe.wait_ge(*q.at("q_ev", hp + 1))
                    if hp >= 4:
                        pe.wait_ge(q["q_tk"], len(blocks_of(EARLY[layer])) * (hp - 3))
                    for j in range(len(blocks_of(EARLY[layer]))):
                        mm = pe.matmul(PS[:, 4 + hp % 4, j * P:(j + 1) * P], qs[:, hp % 2, j * P:(j + 1) * P], skT[:, hp, :], start=True, stop=True)
                    mm.then_inc(q["q_s"], 1)

                queries(0)
                for hp in range(2 * PH):
                    if hp + 1 < 2 * PH:
                        queries(hp + 1)
                    key_scores(hp)
                n += 1
                phase_end(pe, n)
                base = sum(BLOCKS[:layer])

                l0, l1 = LATER[layer]

                def chunk_beside(m):
                    m += layer * (BQC + BMC)
                    chunks = [1] * BQC + [2] * BMC + [1] * BQC
                    pe.wait_ge(s_bfull[m % 2], 16 * sum(chunks[m % 2:m + 1:2]))
                    return bring[:, m % 2, :, :]

                def beside():
                    for hp in range(2 * PH + 1):
                        if hp < 2 * PH:
                            w = chunk_beside(hp * P // BW)
                            if hp >= 2:
                                pe.wait_ge(*q.at("b_ev", hp - 1))
                            at = hp * P % BW
                            for k in range(KD):
                                mm = pe.matmul(PS[:, 2 + hp % 2, 0:l1 - l0], w[:, k, at:at + P], hT[:, k, l0:l1], start=(k == 0), stop=(k == KD - 1))
                            mm.then_inc(q["b_mm"], 1)
                        if hp >= 1:
                            last = hp - 1
                            pe.wait_ge(*q.at("b_ev", last + 1))
                            if last >= 3:
                                pe.wait_ge(q["b_tk"], len(blocks_of((l0, l1))) * (last - 2))
                            for j in range(len(blocks_of((l0, l1)))):
                                mm = pe.matmul(PS[:, 4 + last % 3, j * P:(j + 1) * P], qs2[:, last % 2, j * P:(j + 1) * P], skT[:, last, :],
                                               start=True, stop=True)
                            mm.then_inc(q["b_s"], 1)
                        yield
                    if layer + 1 < DEPTH:
                        for i in range(BMC):
                            w = chunk_beside(BQC + i)
                            if i >= 3:
                                pe.wait_ge(*q.at("m_ev", i - 2))
                            for k in range(KD):
                                mm = pe.matmul(PS[0:2, (2, 3, 7)[i % 3], 0:BW], cond[:, :, k], w[:, k, :], start=(k == 0), stop=(k == KD - 1))
                            mm.then_inc(q["m_mm"], 1)
                            if i % 2:
                                yield

                extra = beside()

                def head(b, h):
                    for k in range(TOPK):
                        if k == HALF:
                            next(extra, None)
                        pe.wait_ge(s_v[k % UR], 16 * ((base + b) * SLOTS // UR + h * TOPK // UR + k // UR + 1))
                        pe.wait_ge(*q.at("g_dg", b * SLOTS + h * TOPK + k + 1))
                        for j in range(2):
                            mm = pe.matmul(PS[:, j, :], dg[:, k % 4, :], vring[:, k % UR, j * 512:(j + 1) * 512],
                                           start=(h == 0 and k == 0), stop=(h == PH - 1 and k == TOPK - 1), skip_group_check=True)
                        mm.then_inc(q["g_vd"], 1)
                    next(extra, None)

                def body(b, first=False):
                    if not first:
                        pe.wait_ge(*q.at("g_y", 2 * b))
                    for h in range(PH):
                        head(b, h)

                body(0, True)
                body(1)
                with pe.Fori(2, nblk - 1) as b:
                    body(b)
                body(nblk - 1)
                n += 1
                phase_end(pe, n)

        @block.vector
        def _(dve):
            ch = Chain(dve, c_dve)
            dve.memset(eps[:, :], EPS).then_inc(s_eps, 1)
            dve.wait_ge(s_const, 2)
            dve.wait_ge(s_load0, 64)
            n = 0
            roots = [0]

            def normalise(dst, src, t):
                return dve.tensor_scalar(dst, src, mv[:, t, 0:1], rstd[:, t:t + 1], ALU.subtract, ALU.mult)

            def all_statistics(layer, count, source):
                parts = []
                for t in range(count):
                    src = source(t)
                    width = src.shape[-1]
                    for j in range(max(1, width // 512)):
                        last = ch.post(dve.bn_stats(st[:, t, j, :], src[:, j * 512:min(width, (j + 1) * 512)]))
                    parts.append((last, j + 1))
                for t, (ready, k) in enumerate(parts):
                    ch.need(ready)
                    last = ch.post(dve.bn_aggr(mv[:, t, :], st[:, t, 0:k, :]))
                ch.need(last)
                ch.sig(dve.tensor_copy(tiny[:, 12:13], mv[:, count - 1, 1:2]), S[layer]["stat"])
                roots[0] += 1
                dve.wait_ge(*S[layer].at("root", roots[0]))
                ch(dve.reciprocal(rstd[:, 0:count], sd[:, 0:count]))

            def scaled(count, view, gain, bias, done):
                ready = [ch.post(normalise(view(t), view(t), t)) for t in range(count)]
                for t in range(count):
                    ch.need(ready[t])
                    ready[t] = ch.post(dve.tensor_tensor(view(t), view(t), gain, ALU.mult))
                for t in range(count):
                    ch.need(ready[t])
                    dve.tensor_tensor(view(t), view(t), bias, ALU.add).then_inc(done, 1)
                    ch.counts[done.name] = ch.counts.get(done.name, 0) + 1
                dve.wait_ge(done, ch.counts[done.name])

            for layer in range(DEPTH):
                q = S[layer]
                nblk = BLOCKS[layer]
                roots[0] = 0
                all_statistics(layer, NB, lambda t: X[:, t, :])

                def modulated(t):
                    s = int(t >= NLAT)
                    if t == 0:
                        dve.wait_ge(*q.at("mbc_in", 64))
                    if t >= 2:
                        dve.wait_ge(*q.at("in_tr", t - 1))
                    ch(normalise(hb[:, t % 2, :], X[:, t, :], t))
                    ch(dve.scalar_tensor_tensor(hb[:, t % 2, :], modbc[:, s, 1, :], 1.0, hb[:, t % 2, :], ALU.add, ALU.mult))
                    dve.tensor_tensor(hb[:, t % 2, :], hb[:, t % 2, :], modbc[:, s, 0, :], ALU.add).then_inc(q["in_h"], 1)

                if layer == 0:
                    dve.wait_ge(*q.at("bmod", 16))
                for i in range(MODC if layer == 0 else 0):
                    dve.wait_ge(*q.at("mod_mm", i + 1))
                    dve.tensor_tensor(modrow[0:2, i * 512:(i + 1) * 512], PS[0:2, i % 2, :], bmod[0:2, i * 512:(i + 1) * 512], ALU.add).then_inc(q["mod_ev"], 1)
                    if i == MODC - 3:
                        modulated(0)
                        modulated(1)
                if layer == 0:
                    n += 1
                    phase_end(dve, n)
                for t in range(0 if layer else 2, NB):
                    modulated(t)
                tiles = in_tiles(layer)
                for i, (c, t) in enumerate(tiles):
                    if in_owner((c, t)) == "dve":
                        dve.wait_ge(*q.at("in_mm", i + 1))
                        ch.sig(dve.tensor_copy(proj[:, t, c * INW:(c + 1) * INW], PS[:, 4 + i % 4, 0:INW]), q["in_evd"])
                dve.wait_ge(q["in_eva"], sum(in_owner(x) == "act" and x[0] < 2 for x in tiles))
                ch(dve.memset(cin, 0.0))
                ch(dve.memset(rstd[:, :], 1.0))
                for t in range(NB):
                    h0 = 0 if t < nblk else NQ
                    w = (NQ + NKV - h0) * HD
                    src = proj[:, t, h0 * HD:(NQ + NKV) * HD]
                    flat = qn.rearrange("p h d -> p (h d)")[:, 0:w]
                    ch(dve.tensor_tensor(flat, src, src, ALU.mult))
                    ch(dve.tensor_reduce(rstd[:, t * 10 + h0:t * 10 + 10], flat.rearrange("p (h d) -> p h d", d=HD), AX_X, ALU.add))
                ch.sig(dve.tensor_copy(tiny[:, 12:13], rstd[:, 0:1]), q["stat"])
                roots[0] += 1
                dve.wait_ge(*q.at("root", roots[0]))
                ch(dve.reciprocal(rstd[:, :], sd[:, :]))
                dve.wait_ge(*q.at("gqk", 32))
                for t in range(NB):
                    h0 = 0 if t < nblk else NQ
                    src = proj[:, t, h0 * HD:(NQ + NKV) * HD].rearrange("p (h d) -> p h d", d=HD)
                    dst = qr[:, t, :].rearrange("p (h d) -> p h d", d=HD)[:, h0:NQ + NKV, :]
                    if h0 == 0:
                        ch(dve.tensor_tensor(qn[:, 0:NQ, :].rearrange("p (j g) d -> p g j d", g=NKV),
                                             src[:, 0:NQ, :].rearrange("p (g j) d -> p g j d", g=NKV),
                                             rstd[:, t * 10:t * 10 + NQ].rearrange("p (g j) -> p g j", g=NKV).unsqueeze(3).to_broadcast([P, NKV, REP, HD]),
                                             ALU.mult))
                    ch(dve.tensor_tensor(qn[:, NQ:NQ + NKV, :], src[:, NQ - h0:NQ + NKV - h0, :],
                                         rstd[:, t * 10 + NQ:t * 10 + 10].unsqueeze(2).to_broadcast([P, NKV, HD]), ALU.mult))
                    if t >= NLAT:
                        ch.sig(dve.tensor_tensor(dst, qn[:, h0:NQ + NKV, :], gqk[:, h0:NQ + NKV, :], ALU.mult), q["at_q"])
                        continue
                    ch(dve.tensor_tensor(qn, qn, gqk, ALU.mult))
                    halves = qn.rearrange("p h (a s f) -> p h a s f", a=2, s=2)
                    rotated = qr[:, t, :].rearrange("p (h a s f) -> p h a s f", h=NQ + NKV, a=2, s=2)
                    x1, x2 = halves[:, :, :, 0, :], halves[:, :, :, 1, :]
                    cs = cosT[:, t, :, :].unsqueeze(1).to_broadcast([P, NQ + NKV, 2, 16])
                    sn = sinT[:, t, :, :].unsqueeze(1).to_broadcast([P, NQ + NKV, 2, 16])
                    va = tA.rearrange("p (h a f) -> p h a f", h=NQ + NKV, a=2)
                    vb = tB.rearrange("p (h a f) -> p h a f", h=NQ + NKV, a=2)
                    ch(dve.tensor_tensor(va, x1, cs, ALU.mult))
                    ch(dve.tensor_tensor(vb, x2, sn, ALU.mult))
                    ch(dve.tensor_tensor(rotated[:, :, :, 0, :], va, vb, ALU.subtract))
                    ch(dve.tensor_tensor(va, x1, sn, ALU.mult))
                    ch(dve.tensor_tensor(vb, x2, cs, ALU.mult))
                    ch.sig(dve.tensor_tensor(rotated[:, :, :, 1, :], va, vb, ALU.add), q["at_q"])
                for t in range(nblk):
                    dve.wait_ge(*q.at("lo_sig", t + 1))
                    dve.tensor_tensor(proj[:, t, A_AT:A_AT + CW], proj[:, t, A_AT:A_AT + CW], proj[:, t, G_AT:G_AT + CW], ALU.mult).then_inc(q["lo_glu"], 1)
                n += 1
                phase_end(dve, n)
                units = att_units(layer)

                def maximum(i):
                    nk = (NB if units[i][0] == 0 else NCTX) * P
                    dve.wait_ge(*q.at("at_s", i + 1))
                    if i >= 4:
                        dve.wait_ge(*q.at("at_exp", i - 3))
                    ch(dve.tensor_reduce(tiny[:, 13:14], PSf[:, (i % 2) * 1024:(i % 2) * 1024 + nk], AX_X, ALU.max))
                    ch.sig(dve.tensor_scalar(tiny[:, i % 4:i % 4 + 1], tiny[:, 13:14], -SCALE, None, ALU.mult), q["at_max"])

                def reciprocal(i):
                    dve.wait_ge(*q.at("at_exp", i + 1))
                    ch.sig(dve.reciprocal(tiny[:, 8 + i % 4:9 + i % 4], tiny[:, 4 + i % 4:5 + i % 4]), q["at_rcp"])

                turns = [(c, s) for c in range(2) for s in range(1 + (nblk == NB))]

                def taps():
                    for tap in range(TAPS):
                        for j, (c, s) in enumerate(turns):
                            t0, t1 = ((0, LAT), (LAT, TOK))[s]
                            src = cin[:, c, 2 * PAD * s + t0 + tap:2 * PAD * s + t1 + tap]
                            acc = cacc[:, c, t0:t1]
                            at = GROUPS + c * (TAPS + 2)
                            wcol = cols[:, at + tap:at + tap + 1]
                            if tap == 0:
                                dve.tensor_scalar(acc, src, wcol, cols[:, at + TAPS:at + TAPS + 1], ALU.mult, ALU.add).then_inc(q["lo_tap"], 1)
                            else:
                                dve.wait_ge(*q.at("lo_tap", (tap - 1) * len(turns) + j + 1))
                                dve.scalar_tensor_tensor(acc, src, wcol, acc, ALU.mult, ALU.add).then_inc(q["lo_tap"], 1)
                            yield

                tap = taps()
                maximum(0)
                for i in range(len(units)):
                    if i + 1 < len(units):
                        maximum(i + 1)
                    for _ in range(len(turns) // 2):
                        next(tap, None)
                    reciprocal(i)
                    for _ in range(len(turns) // 2):
                        next(tap, None)
                for _ in tap:
                    pass
                n += 1
                phase_end(dve, n)
                dve.wait_ge(*q.at("lo_ld", 96))
                dve.wait_ge(*q.at("lo_gelu", nblk))
                all_statistics(layer, nblk, lambda t: proj[:, t, V_AT:V_AT + GW])
                scaled(nblk, lambda t: proj[:, t, V_AT:V_AT + GW], gln[:, 0, :], gln[:, 1, :], q["lo_vn"])
                dve.wait_ge(*q.at("lo_gm", nblk))
                for t in range(nblk):
                    for g in range(GROUPS):
                        u = proj[:, t, U_AT + g * GC:U_AT + (g + 1) * GC]
                        ins = dve.scalar_tensor_tensor(u, PS[:, 4 + t // 2, (t % 2) * GW + g * GC:(t % 2) * GW + (g + 1) * GC], cols[:, g:g + 1], u, ALU.add, ALU.mult)
                        if g < GROUPS - 1:
                            ch.post(ins)
                    ins.then_inc(q["lo_yg"], 1)
                dve.wait_ge(*q.at("lo_cy", nblk))
                all_statistics(layer, nblk, lambda t: cy[:, t, :])
                scaled(nblk, lambda t: cy[:, t, :], cln[:, 0, :], cln[:, 1, :], q["lo_cn"])
                n += 1
                phase_end(dve, n)
                dve.wait_ge(*q.at("mbc_out", 32))
                dve.wait_ge(*q.at("lnbc", 32))
                dve.wait_ge(*q.at("mbc_sc2", 32))
                dve.wait_ge(*q.at("mbc_sh2", 32))

                def block_statistics(t):
                    for j in range(2):
                        dve.bn_stats(st[:, t, j, :], X[:, t, j * 512:(j + 1) * 512]).then_inc(c_dve, 1)
                        ch.n += 1
                    dve.wait_ge(c_dve, ch.n)
                    ch.sig(dve.bn_aggr(mv[:, t, :], st[:, t, :, :]), S[layer]["stat"])
                    roots[0] += 1
                    dve.wait_ge(S[layer]["root"], roots[0])
                    ch(dve.reciprocal(rstd[:, t:t + 1], sd[:, 0:1]))

                for t in range(nblk):
                    s = int(t >= NLAT)
                    for c in range(OUTC):
                        i = t * OUTC + c
                        dve.wait_ge(*q.at("ou_mm", i + 1))
                        cs = slice(c * 512, (c + 1) * 512)
                        ch.sig(dve.tensor_tensor(spare[:, c, :], PS[:, i % 4, :], modbc[:, s, 0, cs], ALU.mult), q["ou_ev"])
                        ch(dve.scalar_tensor_tensor(X[:, t, cs], X[:, t, cs], ALPHA, spare[:, c, :], ALU.mult, ALU.add))
                    block_statistics(t)
                    ch(normalise(X[:, t, :], X[:, t, :], t))
                    ch(dve.tensor_tensor(X[:, t, :], X[:, t, :], lnbc[:, 0, :], ALU.mult))
                    ch(dve.tensor_tensor(X[:, t, :], X[:, t, :], lnbc[:, 1, :], ALU.add))
                    block_statistics(t)
                    ch(normalise(H2[:, place_of(layer, t), :], X[:, t, :], t))
                    ch(dve.scalar_tensor_tensor(H2[:, place_of(layer, t), :], modbc[:, s, 1, :], 1.0, H2[:, place_of(layer, t), :], ALU.add, ALU.mult))
                    ch.sig(dve.tensor_tensor(H2[:, place_of(layer, t), :], H2[:, place_of(layer, t), :], shift2[:, s, :], ALU.add), q["ph_h"])

                n += 1
                phase_end(dve, n)
                def top_keys(src, t, hp, done):
                    where = place_of(layer, t)
                    v = V16[:, where, hp * TOPK:(hp + 1) * TOPK]
                    ix = I16[:, where, hp * TOPK:(hp + 1) * TOPK]
                    ch(dve.max(v[:, 0:8], src))
                    ch(dve.max_index(ix[:, 0:8], v[:, 0:8], src))
                    ch(dve.match_replace(scr[:, :], v[:, 0:8], src, LOWEST))
                    ch(dve.max(v[:, 8:16], scr[:, :]))
                    ch.sig(dve.max_index(ix[:, 8:16], v[:, 8:16], scr[:, :]), done)

                base = sum(BLOCKS[:layer])
                STEPS = 15

                def hold(s, value):
                    dve.wait_ge(s, value)
                    if not isinstance(value, int):
                        dve.sem_inc(s_hold, 1)

                def at(view, b, off, size):
                    if isinstance(b, int):
                        return view[:, b * (view.shape[-1] // NB) + off:b * (view.shape[-1] // NB) + off + size]
                    return view[:, bass.ds(b * (view.shape[-1] // NB) + off, size)]

                def best_experts(b, h):
                    done = [0]
                    origin = (b * PH + h + base * PH) * STEPS

                    def link(ins, apart=False):
                        ins.then_inc(c_tk, 1)
                        done[0] += 1
                        (hold if apart else dve.wait_ge)(c_tk, origin + done[0])

                    v = at(V16f, b, 2 * h * TOPK, 2 * TOPK)
                    ix = at(I16f, b, 2 * h * TOPK, 2 * TOPK)
                    c2 = cand.rearrange("p (i j) -> p i j", i=TOPK)
                    e2 = eq.rearrange("p (i j) -> p i j", i=TOPK)
                    k0 = h * TOPK
                    bst = best[:, k0:k0 + TOPK]

                    def down(x):
                        return x.unsqueeze(2).to_broadcast([P, TOPK, TOPK])

                    def across(x):
                        return x.unsqueeze(1).to_broadcast([P, TOPK, TOPK])

                    link(dve.tensor_tensor(c2, down(v[:, 0:TOPK]), across(v[:, TOPK:2 * TOPK]), ALU.add), True)
                    link(dve.max(bst[:, 0:8], cand), True)
                    link(dve.max_index(pos[:, 0:8], bst[:, 0:8], cand), True)
                    link(dve.match_replace(cand, bst[:, 0:8], cand, LOWEST), True)
                    link(dve.max(bst[:, 8:16], cand), True)
                    link(dve.max_index(pos[:, 8:16], bst[:, 8:16], cand))
                    gt = gate[:, k0:k0 + TOPK]
                    dve.tensor_scalar(gt, bst, bst[:, 0:1], None, ALU.subtract).then_inc(q["g_best"], 1)
                    link(dve.tensor_scalar(hilo[:, 0:TOPK], pos, 4, None, ALU.logical_shift_right))
                    link(dve.tensor_scalar(hilo[:, TOPK:2 * TOPK], pos, TOPK - 1, None, ALU.bitwise_and))
                    for half in range(2):
                        link(dve.tensor_tensor(e2, down(hilo[:, half * TOPK:(half + 1) * TOPK]), across(iota16[:, :]), ALU.is_equal), True)
                        link(dve.tensor_tensor(e2, e2, across(ix[:, half * TOPK:(half + 1) * TOPK]), ALU.mult))
                        link(dve.tensor_reduce(e12[:, half * TOPK:(half + 1) * TOPK], e2, AX_X, ALU.add))
                    link(dve.tensor_scalar(e12[:, 0:TOPK], e12[:, 0:TOPK], float(NK), float(layer * NEXP), ALU.mult, ALU.add))
                    dve.tensor_tensor(idx[:, k0:k0 + TOPK], e12[:, 0:TOPK], e12[:, TOPK:2 * TOPK], ALU.add).then_inc(q["g_idx"], 1)
                    assert done[0] == STEPS, done[0]

                def products(b, h, lo=0, hi=TOPK):
                    for k in range(lo, hi):
                        dve.wait_ge(s_u[k % UR], 16 * ((base + b) * SLOTS // UR + h * TOPK // UR + k // UR + 1))
                        col = (h % PH) * TOPK + k
                        dve.tensor_tensor_reduce(uring[:, k % UR, :], uring[:, k % UR, :], hcur, 1.0, 0.0, ALU.mult, ALU.add,
                                                 actv[:, col:col + 1]).then_inc(q["g_ud"], 1)

                def weigh(b, h):
                    dve.wait_ge(*q.at("g_gel", b * PH + h + 1))
                    dve.reciprocal(tiny[:, 9:10], gsum[:, h:h + 1]).then_inc(c_up, 1)
                    dve.wait_ge(c_up, (base + b) * PH + h + 1)
                    dve.scalar_tensor_tensor(wgt[:, h * TOPK:(h + 1) * TOPK], gel[:, h * TOPK:(h + 1) * TOPK], tiny[:, 9:10],
                                             gate[:, h * TOPK:(h + 1) * TOPK], ALU.mult, ALU.mult).then_inc(q["g_w"], 1)

                def beside():
                    yield
                    yield
                    for hp in range(2 * PH):
                        dve.wait_ge(*q.at("b_s", hp + 1))
                        for j, t in enumerate(blocks_of(LATER[layer])):
                            top_keys(PS[:, 4 + hp % 3, j * P:(j + 1) * P], t, hp, q["b_tk"])
                        yield
                    if layer + 1 < DEPTH:
                        for i in range(BMC):
                            dve.wait_ge(*q.at("m_mm", i + 1))
                            dve.tensor_tensor(modrow2[0:2, i * BW:(i + 1) * BW], PS[0:2, (2, 3, 7)[i % 3], 0:BW], brow[0:2, (BQC + i) % 2, 0:BW],
                                              ALU.add).then_inc(q["m_ev"], 1)
                            if i % 2:
                                yield

                waiting = beside()
                r0 = roots[0]

                def leave(p):
                    t = block_at(layer, p)
                    s = int(t >= NLAT)
                    dve.wait_ge(*q.at("g_y", 2 * (p + 1)))
                    ch(dve.tensor_tensor(H2[:, p, :], H2[:, p, :], gate2[:, s, :], ALU.mult))
                    ch(dve.scalar_tensor_tensor(X[:, t, :], X[:, t, :], ALPHA, H2[:, p, :], ALU.mult, ALU.add))
                    for j in range(2):
                        ch(dve.bn_stats(st[:, p, j, :], X[:, t, j * 512:(j + 1) * 512]))
                    ch.sig(dve.bn_aggr(mv[:, p, :], st[:, p, :, :]), q["stat"])

                def settle(p):
                    t = block_at(layer, p)
                    dve.wait_ge(*q.at("root", r0 + p + 1))
                    ch(dve.reciprocal(rstd[:, p:p + 1], sd[:, p:p + 1]))
                    ch(normalise(X[:, t, :], X[:, t, :], p))
                    ch(dve.tensor_tensor(X[:, t, :], X[:, t, :], lnbc[:, 0, :], ALU.mult))
                    ch.sig(dve.tensor_tensor(X[:, t, :], X[:, t, :], lnbc[:, 1, :], ALU.add), q["ep"])

                def close():
                    for j in range(nblk + 1):
                        if j < nblk - 1:
                            leave(j)
                        if j >= 2:
                            settle(j - 2)
                        yield

                def current(b):
                    if not isinstance(b, int) or b > 0:
                        hold(*q.at("g_ud", b * SLOTS))
                    dve.tensor_copy(hcur, at(H2f, b, 0, D)).then_inc(q["g_h"], 1)
                    dve.wait_ge(*q.at("g_h", b + 1))

                def body(b, last, first=False):
                    extra = close() if last else waiting
                    if last:
                        dve.wait_ge(*q.at("mbc_g2", 32))
                        dve.wait_ge(*q.at("lnbc2", 32))
                    for h in range(1, PH + 1):
                        tops = [(b + ahead, hh) for ahead, hh in top_steps(first)[h] if ahead == 0 or not last]
                        if h == PH and not last:
                            current(b + 1)
                        if h < PH or not last:
                            products(b, h, 0, 4)
                        weigh(b, h - 1)
                        more = h < PH or not last
                        if more:
                            products(b, h, 4, HALF)
                        next(extra, None)
                        if len(tops) == 2:
                            best_experts(*tops[0])
                        if more:
                            products(b, h, HALF, TOPK)
                        next(extra, None)
                        if tops:
                            best_experts(*tops[-1])

                for hp in range(2 * PH):
                    dve.wait_ge(*q.at("q_s", hp + 1))
                    for j, t in enumerate(blocks_of(EARLY[layer])):
                        top_keys(PS[:, 4 + hp % 4, j * P:(j + 1) * P], t, hp, q["q_tk"])
                    if hp in (5, 9):
                        best_experts(0, (hp - 5) // 4)
                current(0)
                n += 1
                phase_end(dve, n)
                products(0, 0)
                body(0, False, True)
                body(1, False)
                with dve.Fori(2, nblk - 1) as b:
                    body(b, False)
                body(nblk - 1, True)
                leave(nblk - 1)
                settle(nblk - 1)
                n += 1
                phase_end(dve, n)


_INS = ['x', 'c', 'ctx', 'c_ctx', 'w_mod', 'b_mod', 'w_in', 'q_norm_g', 'k_norm_g', 'gmlp_ln_g', 'gmlp_ln_b', 'gmlp_w_s', 'gmlp_b_s',
        'conv_w_dw', 'conv_b_dw', 'conv_ln_g', 'conv_ln_b', 'conv_w_pw', 'conv_b_pw', 'w_out', 'ln1_g', 'ln1_b', 'ln2_g', 'ln2_b',
        'peer_w_q', 'peer_sub_keys', 'peer_u', 'peer_v']


def rope_tables():
    import numpy as np
    grid = 64
    half = HD // 4
    freqs = (np.float32(10000.0) ** (-np.arange(half, dtype=np.float32) / np.float32(half))).astype(np.float32)
    where = np.arange(LAT)
    angles = np.stack([(where // grid).astype(np.float32)[:, None] * freqs, (where % grid).astype(np.float32)[:, None] * freqs], 1)
    angles = angles.reshape(LAT, 2 * half).astype(np.float64)
    return np.cos(angles).astype(np.float32), np.sin(angles).astype(np.float32)


def kernel(**inputs):
    import numpy as _np
    import concourse.bacc as _bacc
    from concourse import mybir as _mybir
    from concourse.bass_utils import run_bass_kernel_spmd as _run

    nc = _bacc.Bacc("TRN2", target_bir_lowering=False, num_devices=1)
    arrays, aps = {}, {}
    shaped = {name: inputs[name] for name in _INS}
    for name in ("peer_u", "peer_v"):
        shaped[name] = inputs[name].reshape(DEPTH * NEXP, D)
    shaped["rope_cos"], shaped["rope_sin"] = rope_tables()
    for name, value in shaped.items():
        array = _np.ascontiguousarray(value)
        arrays[f"in_{name}_dram"] = array
        aps[name] = nc.dram_tensor(f"in_{name}_dram", array.shape, _mybir.dt.from_np(array.dtype), kind="ExternalInput").ap()
    out = nc.dram_tensor("out_0_dram", (1, LAT, D), F32, kind="ExternalOutput").ap()
    build(nc, aps, aps["rope_cos"], aps["rope_sin"], out)
    r = _run(nc, [arrays], core_ids=[0])
    return r.results[0]["out_0_dram"]
```
